# Optimizing a Trainium2 kernel written in Bass

```python
import math
import jax, jax.numpy as jnp
from jax import lax
import numpy as np

D_MODEL = 1024
BATCH = 1
SEQ = 256
DEPTH = 2

GRID_W = 64
CTX_LEN = 256
N_HEADS = 8
Q_LORA = 256
KV_LORA = 128
QK_NOPE = 64
QK_ROPE = 32
V_HEAD = 64
ATT_WIDTH = N_HEADS * V_HEAD
ATT_SCALE = (QK_NOPE + QK_ROPE) ** -0.5
ROPE_BASE = 10000.0
Q_BLOCK = 128
FOURIER_WIDTH = 256
POOL_WINDOWS = (2, 4, 8, 16)
POOL_GROUP = 64
POOL_WIDTH = POOL_GROUP * len(POOL_WINDOWS)
N_BRANCH = 3
IN_WIDTH = Q_LORA + KV_LORA + QK_ROPE + FOURIER_WIDTH + POOL_WIDTH + N_BRANCH * D_MODEL
SPLITS = (Q_LORA, Q_LORA + KV_LORA, Q_LORA + KV_LORA + QK_ROPE,
          Q_LORA + KV_LORA + QK_ROPE + FOURIER_WIDTH,
          Q_LORA + KV_LORA + QK_ROPE + FOURIER_WIDTH + POOL_WIDTH)
PEER_HEADS = 8
N_KEYS = 128
N_EXPERTS = N_KEYS * N_KEYS
PEER_QDIM = 256
PEER_TOPK = 16
TOKEN_BLOCK = 128
EPS = 1e-6


def _rmsnorm(x, g):
    xf = x.astype(jnp.float32)
    y = xf * lax.rsqrt(jnp.mean(xf * xf, axis=-1, keepdims=True) + EPS)
    return (y * g.astype(jnp.float32)).astype(x.dtype)

def _modulation(cvec, w_mod, b_mod):
    m = jax.nn.silu(cvec) @ w_mod + b_mod
    return jnp.split(m[:, None, :], 6, axis=-1)

def _modulate(x, g, shift, scale):
    return _rmsnorm(x, g) * (1 + scale) + shift

def _axial_angles(L):
    rows = L // GRID_W
    r, cl = jnp.meshgrid(jnp.arange(rows, dtype=jnp.float32),
                         jnp.arange(GRID_W, dtype=jnp.float32), indexing="ij")
    half = QK_ROPE // 2
    inv_freq = ROPE_BASE ** (-jnp.arange(0, half, 2, dtype=jnp.float32) / half)
    ang_r = r.reshape(L, 1, 1) * inv_freq
    ang_c = cl.reshape(L, 1, 1) * inv_freq
    return ang_r, ang_c

def _rotate_half(x, ang):
    x1, x2 = jnp.split(x.astype(jnp.float32), 2, axis=-1)
    cos, sin = jnp.cos(ang), jnp.sin(ang)
    return jnp.concatenate([x1 * cos - x2 * sin, x1 * sin + x2 * cos], axis=-1)

def _rope_2d(x, ang):
    ang_r, ang_c = ang
    xr, xc = jnp.split(x, 2, axis=-1)
    return jnp.concatenate([_rotate_half(xr, ang_r), _rotate_half(xc, ang_c)], axis=-1).astype(x.dtype)

def _mla_q(cq, lp, ang):
    B, L, _ = cq.shape
    q = (_rmsnorm(cq, lp["q_norm_g"]) @ lp["w_uq"]).reshape(B, L, N_HEADS, QK_NOPE + QK_ROPE)
    q_nope, q_rope = q[..., :QK_NOPE], q[..., QK_NOPE:]
    if ang is not None:
        q_rope = _rope_2d(q_rope, ang)
    return jnp.concatenate([q_nope, q_rope], axis=-1)

def _mla_kv(ckv, kr, lp, ang):
    B, L, _ = ckv.shape
    kv = (_rmsnorm(ckv, lp["kv_norm_g"]) @ lp["w_ukv"]).reshape(B, L, N_HEADS, QK_NOPE + V_HEAD)
    k_nope, v = kv[..., :QK_NOPE], kv[..., QK_NOPE:]
    k_rope = kr[:, :, None, :]
    if ang is not None:
        k_rope = _rope_2d(k_rope, ang)
    k = jnp.concatenate([k_nope, jnp.broadcast_to(k_rope, (B, L, N_HEADS, QK_ROPE))], axis=-1)
    return k, v

def _attend(q, k, v):
    s = jnp.einsum("bqhd,bkhd->bhqk", q, k, preferred_element_type=jnp.float32) * ATT_SCALE
    p = jax.nn.softmax(s, axis=-1).astype(v.dtype)
    return jnp.einsum("bhqk,bkhd->bqhd", p, v)

def _latent_attention(q, k, v, kv_ctx):
    k_ctx, v_ctx = kv_ctx
    k_all = jnp.concatenate([k_ctx, k], axis=1)
    v_all = jnp.concatenate([v_ctx, v], axis=1)
    B, L, H, Dq = q.shape
    nb = L // Q_BLOCK
    qb = jnp.moveaxis(q.reshape(B, nb, Q_BLOCK, H, Dq), 1, 0)
    o = lax.map(lambda qq: _attend(qq, k_all, v_all), qb)
    return jnp.moveaxis(o, 0, 1).reshape(B, L, ATT_WIDTH)

def _fourier_mix(z):
    zf = z.astype(jnp.float32)
    return jnp.real(jnp.fft.fft2(zf, axes=(1, 2), norm="ortho")).astype(z.dtype)

def _pool_mix(z, w_grp, pool_scale):
    B, L, _ = z.shape
    zf = z.astype(jnp.float32)
    cs = jnp.concatenate([jnp.zeros((B, 1, POOL_WIDTH), jnp.float32), jnp.cumsum(zf, axis=1)], axis=1)
    t = jnp.arange(L)
    outs = []
    for gi, w in enumerate(POOL_WINDOWS):
        lo = jnp.clip(t - w // 2, 0, L)
        hi = jnp.clip(t - w // 2 + w, 0, L)
        seg = cs[:, :, gi * POOL_GROUP:(gi + 1) * POOL_GROUP]
        cnt = (hi - lo).astype(jnp.float32)[None, :, None]
        outs.append((seg[:, hi] - seg[:, lo]) / cnt - zf[:, :, gi * POOL_GROUP:(gi + 1) * POOL_GROUP])
    pooled = jnp.concatenate(outs, axis=-1).astype(z.dtype).reshape(B, L, len(POOL_WINDOWS), POOL_GROUP)
    y = jnp.einsum("blgc,gcd->blgd", pooled, w_grp).reshape(B, L, POOL_WIDTH)
    return y * pool_scale

def _token_mix(h, lp, ang, kv_ctx):
    B, L, _ = h.shape
    z = h @ lp["w_in"]
    cq, ckv, kr, zf, zp, zg = jnp.split(z, SPLITS, axis=-1)
    q = _mla_q(cq, lp, ang)
    k, v = _mla_kv(ckv, kr, lp, ang)
    if kv_ctx is None:
        att = _attend(q, k, v).reshape(B, L, ATT_WIDTH)
    else:
        att = _latent_attention(q, k, v, kv_ctx)
    y_a = att @ lp["w_oa"]
    y_b = _fourier_mix(zf) @ lp["w_ob"]
    y_c = _pool_mix(zp, lp["w_grp"], lp["pool_scale"]) @ lp["w_oc"]
    g = jax.nn.sigmoid((zg + lp["b_gate"]).astype(jnp.float32)).astype(h.dtype)
    g_a, g_b, g_c = jnp.split(g, N_BRANCH, axis=-1)
    return (g_a * y_a + g_b * y_b + g_c * y_c) @ lp["w_out"], (k, v)

def _ctx_keys_values(hc, lp):
    z = hc @ lp["w_in"][:, Q_LORA:Q_LORA + KV_LORA + QK_ROPE]
    ckv, kr = z[..., :KV_LORA], z[..., KV_LORA:]
    return _mla_kv(ckv, kr, lp, None)

def _peer(h, w_pq, peer_keys, peer_down, peer_up):
    B, L, D = h.shape
    q = (h @ w_pq).reshape(B, L, PEER_HEADS, 2, PEER_QDIM // 2)
    s = jnp.einsum("blhpd,hpkd->blhpk", q, peer_keys, preferred_element_type=jnp.float32)
    sv, si = lax.top_k(s, PEER_TOPK)
    cand = (sv[..., 0, :, None] + sv[..., 1, None, :]).reshape(B, L, PEER_HEADS, PEER_TOPK * PEER_TOPK)
    cidx = (si[..., 0, :, None] * N_KEYS + si[..., 1, None, :]).reshape(B, L, PEER_HEADS, PEER_TOPK * PEER_TOPK)
    top_s, pos = lax.top_k(cand, PEER_TOPK)
    eidx = jnp.take_along_axis(cidx, pos, axis=-1)
    gate = jax.nn.softmax(top_s, axis=-1)
    T = B * L
    nb = T // TOKEN_BLOCK
    hb = h.reshape(nb, TOKEN_BLOCK, D)
    eb = eidx.reshape(nb, TOKEN_BLOCK, PEER_HEADS * PEER_TOPK)
    gb = gate.reshape(nb, TOKEN_BLOCK, PEER_HEADS * PEER_TOPK)

    def one(args):
        hh, ee, gg = args
        a = jnp.einsum("tkd,td->tk", peer_down[ee], hh, preferred_element_type=jnp.float32)
        act = (gg * jax.nn.gelu(a)).astype(hh.dtype)
        return jnp.einsum("tk,tkd->td", act, peer_up[ee])

    return lax.map(one, (hb, eb, gb)).reshape(B, L, D)

def first_inputs(seed: int = 0) -> dict:
    key = jax.random.key(seed)
    ks = jax.random.split(key, 25)
    D = D_MODEL

    def n(k, shape, s):
        return jax.random.normal(k, shape, jnp.float32) * s

    return {
        "x": n(ks[0], (BATCH, SEQ, D), 1.0),
        "c": n(ks[1], (BATCH, D), 1.0),
        "ctx": n(ks[2], (BATCH, CTX_LEN, D), 1.0),
        "c_ctx": n(ks[3], (D,), 1.0),
        "w_mod": n(ks[4], (DEPTH, D, 6 * D), 0.5 * D ** -0.5),
        "b_mod": n(ks[5], (DEPTH, 6 * D), 0.01),
        "norm1_g": 1.0 + n(ks[6], (DEPTH, D), 0.02),
        "norm2_g": 1.0 + n(ks[7], (DEPTH, D), 0.02),
        "w_in": n(ks[8], (DEPTH, D, IN_WIDTH), D ** -0.5),
        "b_gate": n(ks[9], (DEPTH, N_BRANCH * D), 0.01),
        "q_norm_g": 1.0 + n(ks[10], (DEPTH, Q_LORA), 0.02),
        "w_uq": n(ks[11], (DEPTH, Q_LORA, N_HEADS * (QK_NOPE + QK_ROPE)), Q_LORA ** -0.5),
        "kv_norm_g": 1.0 + n(ks[12], (DEPTH, KV_LORA), 0.02),
        "w_ukv": n(ks[13], (DEPTH, KV_LORA, N_HEADS * (QK_NOPE + V_HEAD)), KV_LORA ** -0.5),
        "w_oa": n(ks[14], (DEPTH, ATT_WIDTH, D), ATT_WIDTH ** -0.5),
        "w_ob": n(ks[15], (DEPTH, FOURIER_WIDTH, D), FOURIER_WIDTH ** -0.5),
        "w_grp": n(ks[16], (DEPTH, len(POOL_WINDOWS), POOL_GROUP, POOL_GROUP), POOL_GROUP ** -0.5),
        "pool_scale": 1.0 + n(ks[17], (DEPTH, POOL_WIDTH), 0.02),
        "w_oc": n(ks[18], (DEPTH, POOL_WIDTH, D), POOL_WIDTH ** -0.5),
        "w_out": n(ks[19], (DEPTH, D, D), D ** -0.5),
        "w_pq": n(ks[20], (DEPTH, D, PEER_HEADS * PEER_QDIM), D ** -0.5),
        "peer_keys": n(ks[21], (DEPTH, PEER_HEADS, 2, N_KEYS, PEER_QDIM // 2), (PEER_QDIM // 2) ** -0.5),
        "peer_down": n(ks[22], (DEPTH, N_EXPERTS, D), D ** -0.5),
        "peer_up": n(ks[23], (DEPTH, N_EXPERTS, D), PEER_HEADS ** -0.5),
        "final_g": 1.0 + n(ks[24], (D,), 0.02),
    }

def first_block(x, c, ctx, c_ctx, w_mod, b_mod, norm1_g, norm2_g, w_in, b_gate, q_norm_g, w_uq,
              kv_norm_g, w_ukv, w_oa, w_ob, w_grp, pool_scale, w_oc, w_out, w_pq, peer_keys,
              peer_down, peer_up, final_g):
    L = x.shape[1]
    ang = _axial_angles(L)
    for l in range(DEPTH):
        last = l == DEPTH - 1
        lp = {"w_in": w_in[l], "b_gate": b_gate[l], "q_norm_g": q_norm_g[l], "w_uq": w_uq[l],
              "kv_norm_g": kv_norm_g[l], "w_ukv": w_ukv[l], "w_oa": w_oa[l], "w_ob": w_ob[l],
              "w_grp": w_grp[l], "pool_scale": pool_scale[l], "w_oc": w_oc[l], "w_out": w_out[l]}
        m_x = _modulation(c, w_mod[l], b_mod[l])
        m_c = _modulation(c_ctx[None, :], w_mod[l], b_mod[l])
        h = _modulate(x, norm1_g[l], m_x[0], m_x[1])
        hc = _modulate(ctx, norm1_g[l], m_c[0], m_c[1])
        if last:
            kv_c = _ctx_keys_values(hc, lp)
        else:
            mix_c, kv_c = _token_mix(hc, lp, None, None)
        mix_x, _ = _token_mix(h, lp, ang, kv_c)
        x = x + m_x[2] * mix_x
        h2 = _modulate(x, norm2_g[l], m_x[3], m_x[4])
        x = x + m_x[5] * _peer(h2, w_pq[l], peer_keys[l], peer_down[l], peer_up[l])
        if not last:
            ctx = ctx + m_c[2] * mix_c
            hc2 = _modulate(ctx, norm2_g[l], m_c[3], m_c[4])
            ctx = ctx + m_c[5] * _peer(hc2, w_pq[l], peer_keys[l], peer_down[l], peer_up[l])
    return _rmsnorm(x, final_g)


DEPTH_2 = 1

HEAD_DIM = 64
ATT_WIDTH_2 = D_MODEL // 2
RWKV_WIDTH = D_MODEL - ATT_WIDTH_2
ATT_HEADS = ATT_WIDTH_2 // HEAD_DIM
RWKV_HEADS = RWKV_WIDTH // HEAD_DIM
MIX_WIDTH = ATT_WIDTH_2 + RWKV_WIDTH
DILATED_PATTERNS = ((128, 1), (512, 4), (2048, 16))
DECAY_LORA = 64
AAA_LORA = 64
GATE_LORA = 128
SHIFT_WIDTH = 3 * RWKV_WIDTH + DECAY_LORA + AAA_LORA + GATE_LORA
IN_WIDTH_2 = 3 * ATT_WIDTH_2 + SHIFT_WIDTH
PEER_N_KEYS = 128
PEER_N_EXPERTS = PEER_N_KEYS * PEER_N_KEYS
PEER_KEY_DIM = 256
PEER_TOKEN_BLOCK = 128
NORM_EPS = 1e-6
LNX_EPS = 64e-5
MASK_VALUE = -1e30


def rms_norm(x, g, eps=NORM_EPS):
    x32 = x.astype(jnp.float32)
    y = x32 * lax.rsqrt(jnp.mean(x32 * x32, axis=-1, keepdims=True) + eps)
    return y * g.astype(jnp.float32)

def alibi_slopes(n_heads):
    return jnp.exp2(-8.0 * (jnp.arange(n_heads, dtype=jnp.float32) + 1.0) / n_heads)

def dilated_window_attention(q, k, v, slopes, window, dilation):
    B, S, H, E = q.shape
    d = dilation
    n = window // (2 * d)
    L = S // d
    nb = -(-L // n)
    Lp = nb * n
    qs = jnp.pad(q.reshape(B, L, d, H, E), ((0, 0), (0, Lp - L), (0, 0), (0, 0), (0, 0)))
    qs = qs.reshape(B, nb, n, d, H, E)

    def neighbourhood(t):
        tp = jnp.pad(t.reshape(B, L, d, H, E), ((0, 0), (n, Lp - L + n), (0, 0), (0, 0), (0, 0)))
        tp = tp.reshape(B, nb + 2, n, d, H, E)
        return jnp.concatenate([tp[:, :-2], tp[:, 1:-1], tp[:, 2:]], axis=2)

    kb = neighbourhood(k)
    vb = neighbourhood(v)
    qi = jnp.arange(nb)[:, None] * n + jnp.arange(n)[None, :]
    kj = (jnp.arange(nb)[:, None] - 1) * n + jnp.arange(3 * n)[None, :]
    off = kj[:, None, :] - qi[:, :, None]
    valid = (jnp.abs(off) <= n) & (kj[:, None, :] >= 0) & (kj[:, None, :] < L)
    dist = (d * jnp.abs(off)).astype(jnp.float32)

    s = jnp.einsum('bnqrhe,bnkrhe->bhrnqk', qs, kb) * (E ** -0.5)
    s = s - slopes[None, :, None, None, None, None] * dist[None, None, None]
    s = jnp.where(valid[None, None, None], s, MASK_VALUE)
    m = jnp.max(s, axis=-1, keepdims=True)
    p = jnp.exp(s - m)
    den = jnp.sum(p, axis=-1)
    lse = m[..., 0] + jnp.log(den)
    out = jnp.einsum('bhrnqk,bnkrhe->bnqrhe', p, vb)
    out = out / jnp.transpose(den, (0, 3, 4, 2, 1))[..., None]
    out = out.reshape(B, Lp, d, H, E)[:, :L].reshape(B, S, H, E)
    lse = jnp.transpose(lse, (0, 3, 4, 2, 1)).reshape(B, Lp, d, H)[:, :L].reshape(B, S, H)
    return out, lse

def dilated_mixture_attention(q, k, v):
    slopes = alibi_slopes(q.shape[2])
    outs, lses = [], []
    for window, dilation in DILATED_PATTERNS:
        o, l = dilated_window_attention(q, k, v, slopes, window, dilation)
        outs.append(o)
        lses.append(l)
    wts = jax.nn.softmax(jnp.stack(lses, axis=0), axis=0)
    return jnp.einsum('pbsh,pbshe->bshe', wts, jnp.stack(outs, axis=0))

def token_shift(z, mu_prev, mu_next):
    z_prev = jnp.pad(z, ((0, 0), (1, 0), (0, 0)))[:, :-1]
    z_next = jnp.pad(z, ((0, 0), (0, 1), (0, 0)))[:, 1:]
    return z + mu_prev * (z_prev - z) + mu_next * (z_next - z)

def wkv7_scan(r, w, k, v, kk, a, reverse):
    B, S, H, N = r.shape
    xs = tuple(jnp.moveaxis(t, 1, 0) for t in (r, w, k, v, kk, a))
    state0 = jnp.zeros((B, H, N, N), jnp.float32)

    def step(state, inp):
        r_t, w_t, k_t, v_t, kk_t, a_t = inp
        sa = jnp.einsum('bhvk,bhk->bhv', state, -kk_t)
        state = (state * w_t[:, :, None, :]
                 + sa[..., :, None] * (kk_t * a_t)[..., None, :]
                 + v_t[..., :, None] * k_t[..., None, :])
        y = jnp.einsum('bhvk,bhk->bhv', state, r_t)
        return state, y

    _, ys = lax.scan(step, state0, xs, reverse=reverse)
    return jnp.moveaxis(ys, 0, 1)

def rwkv7_bidirectional(r, k, v, xw, xa, xg, w_decay0, w_decay_up, a_gate0, a_gate_up,
                        g_up, k_k, k_a, r_k, lnx_g, lnx_b):
    B, S, _ = r.shape

    def hs(t):
        return t.reshape(B, S, RWKV_HEADS, HEAD_DIM)

    g = jax.nn.sigmoid(xg) @ g_up
    kk = hs(k * k_k)
    kk = kk * lax.rsqrt(jnp.maximum(jnp.sum(kk * kk, axis=-1, keepdims=True), 1e-12))
    ys, a_dirs = [], []
    for direction in range(2):
        w = -jax.nn.softplus(-(w_decay0[direction] + jnp.tanh(xw) @ w_decay_up[direction])) - 0.5
        decay = jnp.exp(-jnp.exp(w))
        a = jax.nn.sigmoid(a_gate0[direction] + xa @ a_gate_up[direction])
        k_dir = k * (1.0 + (a - 1.0) * k_a)
        ys.append(wkv7_scan(hs(r), hs(decay), hs(k_dir), hs(v), kk, hs(a), reverse=(direction == 1)))
        a_dirs.append(a)
    y = ys[0] + ys[1]
    mean = jnp.mean(y, axis=-1, keepdims=True)
    var = jnp.mean(jnp.square(y - mean), axis=-1, keepdims=True)
    yn = ((y - mean) * lax.rsqrt(var + LNX_EPS)).reshape(B, S, RWKV_WIDTH) * lnx_g + lnx_b
    k_bonus = hs(k * (1.0 + (0.5 * (a_dirs[0] + a_dirs[1]) - 1.0) * k_a))
    bonus = jnp.sum(hs(r) * k_bonus * r_k, axis=-1, keepdims=True) * hs(v)
    return (yn + bonus.reshape(B, S, RWKV_WIDTH)) * g

def peer_ffn(h, w_query, sub_keys1, sub_keys2, expert_u, expert_v):
    B, S, D = h.shape
    T = B * S
    half = PEER_KEY_DIM // 2
    x = h.reshape(T, D)
    q = (x @ w_query).astype(jnp.float32).reshape(T, PEER_HEADS, PEER_KEY_DIM)
    s1 = jnp.einsum('thd,nd->thn', q[..., :half], sub_keys1.astype(jnp.float32))
    s2 = jnp.einsum('thd,nd->thn', q[..., half:], sub_keys2.astype(jnp.float32))
    v1, i1 = lax.top_k(s1, PEER_TOPK)
    v2, i2 = lax.top_k(s2, PEER_TOPK)
    cand = (v1[..., :, None] + v2[..., None, :]).reshape(T, PEER_HEADS, PEER_TOPK * PEER_TOPK)
    top_s, top_p = lax.top_k(cand, PEER_TOPK)
    e_idx = (jnp.take_along_axis(i1, top_p // PEER_TOPK, axis=-1) * PEER_N_KEYS
             + jnp.take_along_axis(i2, top_p % PEER_TOPK, axis=-1))
    gate = jax.nn.softmax(top_s, axis=-1)
    HK = PEER_HEADS * PEER_TOPK
    nblk = T // PEER_TOKEN_BLOCK
    xb = x.reshape(nblk, PEER_TOKEN_BLOCK, D)
    ib = e_idx.reshape(nblk, PEER_TOKEN_BLOCK, HK)
    gb = gate.reshape(nblk, PEER_TOKEN_BLOCK, HK)

    def block(args):
        xc, ic, gc = args
        u = jnp.take(expert_u, ic, axis=0)
        act = jax.nn.gelu(jnp.einsum('cd,ced->ce', xc, u).astype(jnp.float32), approximate=False)
        vv = jnp.take(expert_v, ic, axis=0)
        return jnp.einsum('ce,ced->cd', (gc * act).astype(vv.dtype), vv)

    y = lax.map(block, (xb, ib, gb))
    return y.reshape(B, S, D)

def second_inputs(seed: int = 0) -> dict:
    key = jax.random.key(seed)
    ks = jax.random.split(key, 32)
    f32 = jnp.float32
    nrm = lambda k, shape, s: jax.random.normal(k, shape, f32) * s
    RW = RWKV_WIDTH
    return {
        "x": nrm(ks[0], (BATCH, SEQ, D_MODEL), 1.0),
        "c": nrm(ks[1], (BATCH, D_MODEL), 1.0),
        "ada_w": nrm(ks[2], (DEPTH_2, D_MODEL, 6 * D_MODEL), 0.5 * D_MODEL ** -0.5),
        "ada_b": nrm(ks[3], (DEPTH_2, 6 * D_MODEL), 0.1),
        "norm1_g": 1.0 + nrm(ks[4], (DEPTH_2, D_MODEL), 0.05),
        "w_in": nrm(ks[5], (DEPTH_2, D_MODEL, IN_WIDTH_2), D_MODEL ** -0.5),
        "mu_prev": jax.random.uniform(ks[6], (DEPTH_2, SHIFT_WIDTH), f32, 0.0, 0.5),
        "mu_next": jax.random.uniform(ks[7], (DEPTH_2, SHIFT_WIDTH), f32, 0.0, 0.5),
        "q_norm_g": 1.0 + nrm(ks[8], (DEPTH_2, HEAD_DIM), 0.05),
        "k_norm_g": 1.0 + nrm(ks[9], (DEPTH_2, HEAD_DIM), 0.05),
        "w_decay0": jax.random.uniform(ks[10], (DEPTH_2, 2, RW), f32, -5.0, -1.0),
        "w_decay_up": nrm(ks[11], (DEPTH_2, 2, DECAY_LORA, RW), 0.5 * DECAY_LORA ** -0.5),
        "a_gate0": nrm(ks[12], (DEPTH_2, 2, RW), 0.5),
        "a_gate_up": nrm(ks[13], (DEPTH_2, 2, AAA_LORA, RW), AAA_LORA ** -0.5),
        "g_up": nrm(ks[14], (DEPTH_2, GATE_LORA, RW), GATE_LORA ** -0.5),
        "k_k": 0.85 + nrm(ks[15], (DEPTH_2, RW), 0.05),
        "k_a": 1.0 + nrm(ks[16], (DEPTH_2, RW), 0.05),
        "r_k": nrm(ks[17], (DEPTH_2, RWKV_HEADS, HEAD_DIM), 0.1),
        "lnx_g": 1.0 + nrm(ks[18], (DEPTH_2, RW), 0.05),
        "lnx_b": nrm(ks[19], (DEPTH_2, RW), 0.01),
        "w_out": nrm(ks[20], (DEPTH_2, MIX_WIDTH, D_MODEL), MIX_WIDTH ** -0.5),
        "norm2_g": 1.0 + nrm(ks[21], (DEPTH_2, D_MODEL), 0.05),
        "peer_w_query": nrm(ks[22], (DEPTH_2, D_MODEL, PEER_HEADS * PEER_KEY_DIM), D_MODEL ** -0.5),
        "peer_sub_keys1": nrm(ks[23], (DEPTH_2, PEER_N_KEYS, PEER_KEY_DIM // 2), (PEER_KEY_DIM // 2) ** -0.5),
        "peer_sub_keys2": nrm(ks[24], (DEPTH_2, PEER_N_KEYS, PEER_KEY_DIM // 2), (PEER_KEY_DIM // 2) ** -0.5),
        "peer_u": nrm(ks[25], (DEPTH_2, PEER_N_EXPERTS, D_MODEL), D_MODEL ** -0.5),
        "peer_v": nrm(ks[26], (DEPTH_2, PEER_N_EXPERTS, D_MODEL), (PEER_HEADS * PEER_TOPK) ** -0.5),
    }

def second_block(x, c, ada_w, ada_b, norm1_g, w_in, mu_prev, mu_next, q_norm_g, k_norm_g,
              w_decay0, w_decay_up, a_gate0, a_gate_up, g_up, k_k, k_a, r_k, lnx_g, lnx_b,
              w_out, norm2_g, peer_w_query, peer_sub_keys1, peer_sub_keys2, peer_u, peer_v):
    in_dtype = x.dtype
    B, S, _ = x.shape
    A = ATT_WIDTH_2
    RW = RWKV_WIDTH
    for l in range(DEPTH_2):
        mod = (jax.nn.silu(c.astype(jnp.float32)) @ ada_w[l].astype(jnp.float32)
               + ada_b[l].astype(jnp.float32))[:, None, :]
        shift1, scale1, gate1, shift2, scale2, gate2 = jnp.split(mod, 6, axis=-1)

        h = rms_norm(x, norm1_g[l]) * (1.0 + scale1) + shift1
        z = (h.astype(in_dtype) @ w_in[l]).astype(jnp.float32)
        qa = rms_norm(z[..., :A].reshape(B, S, ATT_HEADS, HEAD_DIM), q_norm_g[l])
        ka = rms_norm(z[..., A:2 * A].reshape(B, S, ATT_HEADS, HEAD_DIM), k_norm_g[l])
        va = z[..., 2 * A:3 * A].reshape(B, S, ATT_HEADS, HEAD_DIM)
        att = dilated_mixture_attention(qa, ka, va).reshape(B, S, A)

        zr = token_shift(z[..., 3 * A:], mu_prev[l].astype(jnp.float32), mu_next[l].astype(jnp.float32))
        o1, o2, o3 = RW, 2 * RW, 3 * RW
        o4, o5 = o3 + DECAY_LORA, o3 + DECAY_LORA + AAA_LORA
        rw = rwkv7_bidirectional(
            zr[..., :o1], zr[..., o1:o2], zr[..., o2:o3],
            zr[..., o3:o4], zr[..., o4:o5], zr[..., o5:],
            w_decay0[l].astype(jnp.float32), w_decay_up[l].astype(jnp.float32),
            a_gate0[l].astype(jnp.float32), a_gate_up[l].astype(jnp.float32),
            g_up[l].astype(jnp.float32), k_k[l].astype(jnp.float32), k_a[l].astype(jnp.float32),
            r_k[l].astype(jnp.float32), lnx_g[l].astype(jnp.float32), lnx_b[l].astype(jnp.float32))
        mixed = jnp.concatenate([att, rw], axis=-1).astype(in_dtype) @ w_out[l]
        x = (x.astype(jnp.float32) + gate1 * mixed.astype(jnp.float32)).astype(in_dtype)

        h2 = (rms_norm(x, norm2_g[l]) * (1.0 + scale2) + shift2).astype(in_dtype)
        ff = peer_ffn(h2, peer_w_query[l], peer_sub_keys1[l], peer_sub_keys2[l], peer_u[l], peer_v[l])
        x = (x.astype(jnp.float32) + gate2 * ff.astype(jnp.float32)).astype(in_dtype)
    return x


def setup_inputs(seed=0):
    out = dict(first_inputs(seed))
    for name, value in second_inputs(seed + 1).items():
        if name != "x":
            out[name + "_2"] = value
    return out


def reference(
    x, c, ctx, c_ctx, w_mod, b_mod, norm1_g, norm2_g, w_in, b_gate, q_norm_g, w_uq, kv_norm_g,
    w_ukv, w_oa, w_ob, w_grp, pool_scale, w_oc, w_out, w_pq, peer_keys, peer_down, peer_up,
    final_g, c_2, ada_w_2, ada_b_2, norm1_g_2, w_in_2, mu_prev_2, mu_next_2, q_norm_g_2,
    k_norm_g_2, w_decay0_2, w_decay_up_2, a_gate0_2, a_gate_up_2, g_up_2, k_k_2, k_a_2, r_k_2,
    lnx_g_2, lnx_b_2, w_out_2, norm2_g_2, peer_w_query_2, peer_sub_keys1_2, peer_sub_keys2_2,
    peer_u_2, peer_v_2,
):
    x = first_block(
        x, c, ctx, c_ctx, w_mod, b_mod, norm1_g, norm2_g, w_in, b_gate, q_norm_g, w_uq,
        kv_norm_g, w_ukv, w_oa, w_ob, w_grp, pool_scale, w_oc, w_out, w_pq, peer_keys,
        peer_down, peer_up, final_g,
    )
    return second_block(
        x, c_2, ada_w_2, ada_b_2, norm1_g_2, w_in_2, mu_prev_2, mu_next_2, q_norm_g_2,
        k_norm_g_2, w_decay0_2, w_decay_up_2, a_gate0_2, a_gate_up_2, g_up_2, k_k_2, k_a_2,
        r_k_2, lnx_g_2, lnx_b_2, w_out_2, norm2_g_2, peer_w_query_2, peer_sub_keys1_2,
        peer_sub_keys2_2, peer_u_2, peer_v_2,
    )


_drawn_inputs = setup_inputs


def setup_inputs(seed=0):
    import zlib

    import numpy as np

    out = dict(_drawn_inputs(seed))
    spreads = {}
    factors = {'ctx': 3.729,
     'b_mod': 3.685,
     'norm1_g': 5.989,
     'norm2_g': 4.273,
     'b_gate': 8.0,
     'q_norm_g': 8.0,
     'kv_norm_g': 8.0,
     'pool_scale': 7.913,
     'final_g': 2.793,
     'norm1_g_2': 4.937,
     'q_norm_g_2': 8.0,
     'k_norm_g_2': 8.0,
     'w_decay_up_2': 7.856,
     'k_k_2': 5.664,
     'k_a_2': 4.375,
     'lnx_g_2': 8.0,
     'lnx_b_2': 33.274,
     'norm2_g_2': 8.0,
     'peer_w_query_2': 3.573,
     'peer_sub_keys1_2': 3.729,
     'peer_sub_keys2_2': 3.695,
     'peer_u_2': 4.027,
     'peer_v_2': 3.595}
    for name, (base, spread) in spreads.items():
        noise = np.random.default_rng([zlib.crc32(name.encode()), seed]).standard_normal(out[name].shape)
        drawn = base * np.exp(spread * noise) if base else spread * noise
        out[name] = __import__('jax').numpy.asarray(drawn.astype(out[name].dtype))
    for name, factor in factors.items():
        out[name] = (out[name] * factor).astype(out[name].dtype)
    return out
```

```python
import math
import numpy as np
import concourse.bass as bass
import concourse.mybir as mybir
from contextlib import ExitStack

F32 = mybir.dt.float32
U32 = mybir.dt.uint32
I32 = mybir.dt.int32
ALU = mybir.AluOpType
ACT = mybir.ActivationFunctionType
AX = mybir.AxisListType.X

D = 1024
NEG = -3.0e38
ATT_SCALE = 96 ** -0.5
WINDOWS = (2, 4, 8, 16)
PATTERNS = ((128, 1), (512, 4), (2048, 16))
C16 = 16


def const_tables():
    t = np.arange(256)
    i = np.arange(128)
    c = {}
    c["ident"] = np.eye(128)
    c["iota"] = np.tile(np.arange(16.0), (128, 1))

    def halves(m):
        return m.reshape(2, 128, -1).transpose(1, 0, 2)

    a = 2.0 * np.pi * ((t[:, None] * t[None, :]) % 256) / 256.0
    c["cos"] = halves(np.cos(a) / 16.0)
    c["sin"] = halves(np.sin(a) / 16.0)
    pool = np.zeros((4, 256, 256))
    for g, w in enumerate(WINDOWS):
        lo, hi = np.clip(t - w // 2, 0, 256), np.clip(t - w // 2 + w, 0, 256)
        for u in range(256):
            pool[g, lo[u]:hi[u], u] = 1.0 / (hi[u] - lo[u])
        pool[g] -= np.eye(256)
    c["pool"] = np.stack([halves(p) for p in pool], 1)
    freq = np.float32(10000.0) ** (-np.arange(0, 16, 2, dtype=np.float32) / np.float32(16))
    ang = np.stack([(t // 64)[:, None] * freq, (t % 64)[:, None] * freq], 1).astype(np.float32)
    c["rcos"] = np.cos(ang).reshape(2, 128, 16).transpose(1, 0, 2)
    c["rsin"] = np.sin(ang).reshape(2, 128, 16).transpose(1, 0, 2)
    d = np.abs(t[:, None] - t[None, :])
    n = np.zeros((256, 256))
    for w, dil in PATTERNS:
        n += (d % dil == 0) & (d // dil <= w // (2 * dil))
    c["dist"] = halves(-d.astype(np.float64))
    c["lcnt"] = halves(np.where(n > 0, np.log(np.maximum(n, 1)), -1e30))
    blk = (i[:, None] // 16) == (i[None, :] // 16)
    le, lt = i[:, None] <= i[None, :], i[:, None] < i[None, :]
    c["tri"] = np.stack([blk & le, blk & le.T, blk & lt, blk & lt.T], 1)
    c["msk"] = np.stack([blk & lt.T, blk & lt, blk & le.T, blk & le], 1)
    h, s = i // 16, i % 16
    sel = np.zeros((8, 128, 128))
    for q in range(8):
        sel[q, i, 16 * q + s] = 1.0
    c["sel"] = sel.transpose(1, 0, 2)
    c["selT"] = sel.transpose(2, 0, 1)
    c["hblk"] = (h[:, None] == np.arange(8)[None, :])
    return {k: np.ascontiguousarray(v.reshape(128, -1), dtype=np.float32) for k, v in c.items()}


GROUP0 = ("ident", "iota")
GROUP1 = ("cos", "sin", "pool", "rcos", "rsin")
GROUP2 = ("dist", "lcnt", "tri", "msk", "sel", "selT", "hblk")
WIDTH = {"ident": 128, "iota": 16, "cos": 512, "sin": 512, "pool": 2048, "rcos": 32, "rsin": 32,
         "dist": 512, "lcnt": 512, "tri": 512, "msk": 512, "sel": 1024, "selT": 1024, "hblk": 8}


class Queue:

    def __init__(self, sem, chained):
        self.sem, self.items, self.n, self.chained, self.fence = sem, [], 0, chained, ()

    def last(self):
        return (self.sem, self.n)

    def __call__(self, fn, *after, free=False):
        own = (self.last(),) if self.chained and not free and self.n else ()
        self.items.append(((after, own, self.fence), fn, self.sem, 1))
        self.fence = ()
        self.n += 1
        return (self.sem, self.n)

    def dma(self, cell, out, in_, *after, **kw):
        self.items.append(((after, self.fence), lambda e: e.dma_start(out, in_, **kw), cell.sem, 16))
        self.fence = ()
        cell.n += 16
        return (cell.sem, cell.n)

    def gather(self, cell, out, table, idx, *after):
        self.items.append(((after, self.fence), lambda e: e.indirect_dma_start(
            out=out, out_offset=None, in_=table,
            in_offset=bass.IndirectOffsetOnAxis(ap=idx, axis=0)), cell.sem, 16))
        self.fence = ()
        cell.n += 16
        return (cell.sem, cell.n)

    def hold(self, *tokens):
        self.fence = self.fence + tokens

    def play(self, eng):
        seen = {}

        def wait(t):
            if not t:
                return
            if isinstance(t[0], (tuple, list)) or t[0] is None:
                for u in t:
                    if u is not None:
                        wait(u)
                return
            sem, v = t
            if v and seen.get(id(sem), 0) < v:
                eng.wait_ge(sem, v)
                seen[id(sem)] = v

        for after, fn, sem, inc in self.items:
            wait(after)
            fn(eng).then_inc(sem, inc)


class Cell:

    def __init__(self, sem):
        self.sem, self.n = sem, 0


class Slot:

    def __init__(self, ap, cell=None):
        self.ap, self.cell, self.rel = ap, cell, ()


def program(nc, A, out, dbg):
    ctx = ExitStack()
    with ctx:
        def sem(name):
            return ctx.enter_context(nc.semaphore(name))

        V = Queue(sem("s_vector"), True)
        S = Queue(sem("s_scalar"), True)
        P = Queue(sem("s_tensor"), False)
        G = Queue(sem("s_gpsimd"), True)
        Y = Queue(sem("s_sync"), False)

        def fence(*queues):
            marks = [q.last() for q in (V, S, P, G)]
            for q in queues or (V, S, P, G):
                q.hold(*marks)
            return tuple(marks)

        NB = 52800
        arena = ctx.enter_context(nc.sbuf_tensor("arena", [128, NB], F32))
        pos = [0]

        def buf(*shape, dt=F32):
            n = int(np.prod(shape))
            a = arena[:, pos[0]:pos[0] + n]
            pos[0] += n
            assert pos[0] <= NB, pos[0]
            if dt is not F32:
                a = a.bitcast(dt)
            if len(shape) == 2:
                a = a.rearrange("p (a b) -> p a b", b=shape[1])
            elif len(shape) == 3:
                a = a.rearrange("p (a b c) -> p a b c", b=shape[1], c=shape[2])
            elif len(shape) == 4:
                a = a.rearrange("p (a b c d) -> p a b c d", b=shape[1], c=shape[2], d=shape[3])
            return a

        banks = [Slot(ctx.enter_context(nc.psum_tensor(f"ps{i}", [128, 512], F32))[:, :]) for i in range(8)]
        turn = [0]
        ring_banks = [list(range(8))]

        def bank():
            r = ring_banks[0]
            turn[0] += 1
            return banks[r[turn[0] % len(r)]]

        def mm(o, l, r, start, stop, *after):
            return P(lambda e: e.matmul(o, l, r, start=start, stop=stop), *after)

        def tr(o, i, *after):
            return P(lambda e: e.transpose(o, i, ident), *after)

        def tt(o, a, b, op, *after, q=None, **kw):
            return (q or V)(lambda e: e.tensor_tensor(o, a, b, op), *after, **kw)

        def ts(o, a, s1, s2, op0, op1, *after, q=None, **kw):
            if s2 is None:
                return (q or V)(lambda e: e.tensor_scalar(o, a, s1, None, op0), *after, **kw)
            return (q or V)(lambda e: e.tensor_scalar(o, a, s1, s2, op0, op1), *after, **kw)

        def stt(o, a, s, b, op0, op1, *after, accum=None, **kw):
            return V(lambda e: e.scalar_tensor_tensor(o, a, s, b, op0, op1, accum_out=accum), *after, **kw)

        def act(o, i, f, *after, scale=1.0, bias=0.0, accum=None, **kw):
            return S(lambda e: e.activation(o, i, f, bias=bias, scale=scale, accum_out=accum), *after, **kw)

        def copy(o, i, *after, q=None):
            if q is V:
                return V(lambda e: e.tensor_copy(o, i), *after)
            return act(o, i, ACT.Copy, *after)

        def red(o, i, op, *after):
            return V(lambda e: e.tensor_reduce(o, i, AX, op), *after)

        def recip(o, i, *after):
            return V(lambda e: e.reciprocal(o, i), *after)

        def memset(q, o, v, *after):
            return q(lambda e: e.memset(o, v), *after)

        M, AD, SU = ALU.mult, ALU.add, ALU.subtract

        XR = buf(2, D)
        K0 = buf(144)
        ident, iota = K0[:, 0:128], K0[:, 128:144]
        small = buf(64)
        cv = buf(8, 3)
        svb = buf(8, 3)
        WR = pos[0]
        wslots = [Slot(buf(4096), Cell(sem(f"s_w{i}"))) for i in range(3)]
        wturn = [0]

        def wload(parts, *after):
            s = wslots[wturn[0] % 3]
            wturn[0] += 1
            for f, src in parts:
                t = Y.dma(s.cell, f(s.ap), src, s.rel, after)
            s.tok = t
            return s

        def wblock(src, c0, n):
            v = src[:, c0:c0 + n].rearrange("(k p) n -> p k n", p=128)
            s = wload([(lambda a: a[:, 0:8 * n].rearrange("p (k n) -> p k n", n=n), v)])
            s.w = s.ap[:, 0:8 * n].rearrange("p (k n) -> p k n", n=n)
            return s

        cell0 = Cell(sem("s_const"))
        csm = [Cell(sem(f"s_m{i}")) for i in range(8)]
        cout = Cell(sem("s_out"))
        cdbg = Cell(sem("s_dbg")) if dbg is not None else None

        def dump(name, ap):
            if dbg is None or name not in dbg:
                return
            marks = fence()
            t = Y.dma(cdbg, dbg[name], ap, marks, (cdbg.sem, cdbg.n))
            for q in (V, S, P, G):
                q.hold(t)

        t_id = Y.dma(cell0, K0, A["k0"])
        t_cv = Y.dma(cell0, cv, A["cvec"].rearrange("p (k n) -> p k n", n=3))
        BASE = pos[0]

        modd = nc.dram_tensor("mod_scratch", (5, 6144), F32, kind="Internal").ap()
        silu_t = act(svb, cv, ACT.Sigmoid, t_cv)
        silu_t = tt(svb, svb, cv, M, silu_t)
        bms = [Slot(buf(6144), csm[0]), Slot(buf(6144), csm[1])]
        mds = [Slot(buf(6144), csm[2]), Slot(buf(6144), csm[3])]
        mod_tok = []
        for l in range(3):
            m = 2 if l < 2 else 1
            bm, md = bms[l % 2], mds[l % 2]
            src = A["w_mod"][l] if l < 2 else A["ada_w_2"][0]
            bsrc = (A["b_mod"][l:l + 1, :] if l < 2 else A["ada_b_2"][0:1, :])
            for r in range(m):
                tb = S.dma(bm.cell, bm.ap[r:r + 1, :], bsrc, bm.rel)
            for j in range(12):
                v = src[:, 512 * j:512 * j + 512].rearrange("(p k) n -> p k n", k=8)
                s = wload([(lambda a: a.rearrange("p (k n) -> p k n", n=512), v)])
                w = s.ap.rearrange("p (k n) -> p k n", n=512)
                b = bank()
                for k in range(8):
                    c0 = 0 if l < 2 else 2
                    t = mm(b.ap[0:m, :], svb[:, k, c0:c0 + m], w[:, k, :], k == 0, k == 7, s.tok, silu_t, b.rel)
                s.rel = t
                b.rel = tt(md.ap[0:m, 512 * j:512 * j + 512], b.ap[0:m, :],
                           bm.ap[0:m, 512 * j:512 * j + 512], AD, t, tb, md.rel)
            bm.rel = b.rel
            mod_tok.append(S.dma(md.cell, modd[2 * l:2 * l + m, :], md.ap[0:m, :], b.rel))
            md.rel = mod_tok[-1]
        for q in (V, S, P, G, Y):
            q.hold(*mod_tok)
        fence()
        Y.hold(V.last(), P.last())

        def norm_stat(x, o, w, *after, junk):
            t = act(junk, x, ACT.Square, *after, accum=o)
            t = ts(o, o, 1.0 / w, 1e-6, M, AD, t)
            t = act(o, o, ACT.Sqrt, t)
            return recip(o, o, t)

        pos[0] = BASE
        CR = buf(2, D)
        KC = buf(sum(WIDTH[k] for k in GROUP1))
        kv_ = {}
        o = 0
        for k in GROUP1:
            kv_[k] = KC[:, o:o + WIDTH[k]]
            o += WIDTH[k]
        kcos = kv_["cos"].rearrange("p (k n) -> p k n", n=256)
        ksin = kv_["sin"].rearrange("p (k n) -> p k n", n=256)
        kpool = kv_["pool"].rearrange("p (g k n) -> p g k n", g=4, k=2)
        krc = kv_["rcos"].rearrange("p (t a e) -> p t a e", t=2, a=2)
        krs = kv_["rsin"].rearrange("p (t a e) -> p t a e", t=2, a=2)
        cols = buf(29)
        KE = buf(2048)
        HT = buf(8, 512)
        H2 = buf(4, D)
        bcs = [Slot(buf(D), csm[4 + i]) for i in range(4)]
        STAGE = pos[0]

        def X(t):
            return XR[:, t, :] if t < 2 else CR[:, t - 2, :]

        t_x = None
        cx = Cell(sem("s_x"))
        for t in range(2):
            t_x = S.dma(cx, XR[:, t, :], A["x"][0, 128 * t:128 * t + 128, :])
            t_x = S.dma(cx, CR[:, t, :], A["ctx"][0, 128 * t:128 * t + 128, :], fence())
        t_x = S.dma(cx, KC, A["k1"])
        tok_x = [t_x]

        bturn = [0]

        def brow(src, *after):
            s = bcs[bturn[0] % 4]
            bturn[0] += 1
            s.tok = S.dma(s.cell, s.ap, src.partition_broadcast(128), s.rel, after)
            return s

        def mrow(l, who, i):
            return brow(modd[2 * l + who, 1024 * i:1024 * i + 1024], *mod_tok)

        def modulate(l, g, i0, tiles, *after):
            last = {}
            for who in sorted({t // 2 for t in tiles}):
                gr = brow(g)
                sc = mrow(l, who, i0 + 1)
                sh = mrow(l, who, i0)
                tg = stt(gr.ap, sc.ap, 1.0, gr.ap, AD, M, gr.tok, sc.tok)
                sc.rel = tg
                for t in [t for t in tiles if t // 2 == who]:
                    a = norm_stat(X(t), small[:, t:t + 1], D, *after, tok_x, junk=H2[:, t, :])
                    a = stt(H2[:, t, :], X(t), small[:, t:t + 1], gr.ap, M, M, a)
                    a = tt(H2[:, t, :], H2[:, t, :], sh.ap, AD, sh.tok)
                    for j in range(2):
                        b = bank()
                        for i in range(4):
                            u = tr(b.ap[:, 128 * i:128 * i + 128], H2[:, t, 512 * j + 128 * i:512 * j + 128 * i + 128], a, b.rel)
                        b.rel = copy(HT[:, 4 * j:4 * j + 4, 128 * t:128 * t + 128],
                                     b.ap.rearrange("p (i n) -> p i n", n=128), u, q=(V, S)[j])
                        last[j] = b.rel
                gr.rel = sh.rel = a
            return tuple(last.values())

        def tok_major(s, n, dst, tiles, *after):
            for i, t in enumerate(tiles):
                b = bank()
                for k in range(8):
                    u = mm(b.ap[:, 0:n], HT[:, k, 128 * t:128 * t + 128], s.w[:, k, 0:n], k == 0, k == 7, s.tok, after, b.rel)
                b.rel = copy(dst(t), b.ap[:, 0:n], u, q=(V, S)[i % 2])
            s.rel = u

        gsem = [Cell(sem(f"s_g{i}")) for i in range(16)]

        def peer(l, wq, table_d, table_u, base, tiles, gelu, shared, gate_rows, kex, t_ht, tk):
            T = 128 * len(tiles)
            pos[0] = kex
            EI = buf(4, 128, dt=I32)
            GT = buf(4, 128)
            p0 = pos[0]
            qTs = [Slot(buf(4, 512)) for _ in range(2)]
            SV = buf(4, 16, 16)
            SI = buf(4, 16, 16, dt=U32)
            SF = buf(4, 16, 16)
            tmp = buf(128)
            CA = buf(8, 256)
            TS_ = buf(8, 16)
            TP = buf(8, 16, dt=U32)
            TI = buf(2, 8, 16, dt=U32)
            TF = buf(2, 8, 16)
            EQ = buf(2, 8, 16, 16)
            ES = buf(2, 8, 16)
            sm8 = buf(8)
            sm8b = buf(8)
            for blk in range(4):
                s = wblock(wq, 512 * blk, 512)
                qs = qTs[blk % 2]
                for j in range(4):
                    b = bank()
                    for k in range(8):
                        u = mm(b.ap[:, 0:T], s.w[:, k, 128 * j:128 * j + 128], HT[:, k, 0:T], k == 0, k == 7, s.tok, b.rel, t_ht)
                    tq = b.rel = copy(qs.ap[:, j, 0:T], b.ap[:, 0:T], u, qs.rel, q=S)
                s.rel = u
                for i, t in enumerate(tiles):
                    b = bank()
                    for j in range(4):
                        hp = 4 * blk + j
                        kt = KE[:, 128 * (hp % 2):128 * (hp % 2) + 128] if shared else KE[:, 128 * hp:128 * hp + 128]
                        u = mm(b.ap[:, 128 * j:128 * j + 128], qs.ap[:, j, 128 * i:128 * i + 128], kt, True, True, tq, tk, b.rel)
                    qs.rel = u
                    for j in range(4):
                        hp = 4 * blk + j
                        sc = b.ap[:, 128 * j:128 * j + 128]
                        v1, v2 = SV[:, i, hp, 0:8], SV[:, i, hp, 8:16]
                        i1, i2 = SI[:, i, hp, 0:8], SI[:, i, hp, 8:16]
                        V(lambda e, v1=v1, sc=sc: e.max(v1, sc), u)
                        V(lambda e, v1=v1, sc=sc, i1=i1: e.max_index(i1, v1, sc))
                        V(lambda e, v1=v1, sc=sc: e.match_replace(tmp, v1, sc, NEG))
                        b.rel = V.last()
                        V(lambda e, v2=v2: e.max(v2, tmp))
                        V(lambda e, v2=v2, i2=i2: e.max_index(i2, v2, tmp))
            for i, t in enumerate(tiles):
                V(lambda e, i=i: e.tensor_copy(SF[:, i, :, :], SI[:, i, :, :]))
                sv = SV[:, i, :, :].rearrange("p (h s) k -> p h s k", s=2)
                sf = SF[:, i, :, :].rearrange("p (h s) k -> p h s k", s=2)
                ca = CA.rearrange("p h (a b) -> p h a b", b=16)
                tt(ca, sv[:, :, 0, :].unsqueeze(3).to_broadcast([128, 8, 16, 16]),
                   sv[:, :, 1, :].unsqueeze(2).to_broadcast([128, 8, 16, 16]), AD)
                for h in range(8):
                    c_ = CA[:, h, :]
                    v1, v2, i1, i2 = TS_[:, h, 0:8], TS_[:, h, 8:16], TP[:, h, 0:8], TP[:, h, 8:16]
                    V(lambda e, v1=v1, c_=c_: e.max(v1, c_))
                    V(lambda e, v1=v1, c_=c_, i1=i1: e.max_index(i1, v1, c_))
                    V(lambda e, v1=v1, c_=c_: e.match_replace(c_, v1, c_, NEG))
                    V(lambda e, v2=v2, c_=c_: e.max(v2, c_))
                    V(lambda e, v2=v2, c_=c_, i2=i2: e.max_index(i2, v2, c_))
                ts(TI[:, 0, :, :], TP, 4, None, ALU.logical_shift_right, None)
                ts(TI[:, 1, :, :], TP, 15, None, ALU.bitwise_and, None)
                V(lambda e: e.tensor_copy(TF, TI))
                for s_ in range(2):
                    tt(EQ[:, s_, :, :, :], TF[:, s_, :, :].unsqueeze(3).to_broadcast([128, 8, 16, 16]),
                       iota.unsqueeze(1).unsqueeze(1).to_broadcast([128, 8, 16, 16]), ALU.is_equal)
                    tt(EQ[:, s_, :, :, :], EQ[:, s_, :, :, :], sf[:, :, s_, :].unsqueeze(2).to_broadcast([128, 8, 16, 16]), M)
                    red(ES[:, s_, :, :], EQ[:, s_, :, :, :], AD)
                stt(ES[:, 0, :, :], ES[:, 0, :, :], 128.0, ES[:, 1, :, :], M, AD)
                if base:
                    ts(ES[:, 0, :, :], ES[:, 0, :, :], float(base), None, AD, None)
                V(lambda e, i=i: e.tensor_copy(EI[:, i, :], ES[:, 0, :, :].rearrange("p h k -> p (h k)")))
                gt = GT[:, i, :].rearrange("p (h k) -> p h k", k=16)
                t1 = tt(gt, TS_, TS_[:, :, 0:1].to_broadcast([128, 8, 16]), SU)
                t1 = act(gt, gt, ACT.Exp, t1)
                red(sm8, gt, AD, t1)
                recip(sm8b, sm8)
                tt(gt, gt, sm8b.unsqueeze(2).to_broadcast([128, 8, 16]), M)
            fence()
            pos[0] = p0
            ND = NU = 8
            ht = [HT[:, 2 * i:2 * i + 2, :].rearrange("p a b -> p (a b)") for i in range(4)]
            ds = [Slot(ht[i] if i < 4 else buf(D), gsem[i]) for i in range(ND)]
            us = [Slot(buf(D), gsem[8 + i]) for i in range(NU)]
            dg = [Slot(buf(128)) for _ in range(4)]
            AA = [Slot(buf(128)) for _ in range(2)]
            GA = buf(128)
            AW = [Slot(buf(128)) for _ in range(2)]
            tp = [buf(D) for _ in range(2)]
            GK = 16
            NG = 128 // GK
            steps = [(i, g) for i in range(len(tiles)) for g in range(NG)]
            state = {}
            nd = nu = ng = 0

            def ups(i, g):
                nonlocal nu, ng
                acc = (banks[4], banks[5]) if i % 2 == 0 else (banks[6], banks[7])
                for k in range(GK * g, GK * g + GK):
                    u_ = us[nu % NU]
                    nu += 1
                    tu = G.gather(u_.cell, u_.ap, table_u, EI[:, i, k:k + 1].bitcast(U32), u_.rel)
                    d_ = dg[ng % 4]
                    ng += 1
                    td = act(d_.ap, ident, ACT.Copy, state[i, g], d_.rel, scale=AW[i % 2].ap[:, k:k + 1], free=True)
                    for c in range(2):
                        x = mm(acc[c].ap, d_.ap, u_.ap[:, 512 * c:512 * c + 512], k == 0, k == 127, td, tu, acc[c].rel)
                    u_.rel = d_.rel = x
                AW[i % 2].rel = x
                if g == NG - 1:
                    gr = gate_rows[tiles[i] // 2]
                    X_ = X(tiles[i])
                    for c in range(2):
                        cs = slice(512 * c, 512 * c + 512)
                        a = tt(tp[i % 2][:, cs], acc[c].ap, gr.ap[:, cs], M, x, gr.tok)
                        acc[c].rel = a
                        tt(X_[:, cs], X_[:, cs], tp[i % 2][:, cs], AD)
                    gr.rel = a

            for n, (i, g) in enumerate(steps):
                hp_ = (banks[0], banks[1]) if i % 2 == 0 else (banks[2], banks[3])
                if g == 0:
                    for c in range(2):
                        th = copy(hp_[c].ap, H2[:, tiles[i], 512 * c:512 * c + 512], hp_[c].rel, q=S)
                    AA[i % 2].th = th
                for k in range(GK * g, GK * g + GK):
                    d_ = ds[nd % ND]
                    nd += 1
                    tg = G.gather(d_.cell, d_.ap, table_d, EI[:, i, k:k + 1].bitcast(U32), d_.rel)
                    a = None
                    for c in range(2):
                        cs = slice(512 * c, 512 * c + 512)
                        acc_ = (AA[i % 2].ap if c == 0 else GA)[:, k:k + 1]
                        a = stt(d_.ap[:, cs], d_.ap[:, cs], 1.0, hp_[c].ap, M, M, tg, AA[i % 2].th, AA[i % 2].rel if c == 0 else None,
                                accum=acc_, free=True)
                    d_.rel = a
                hp_[0].rel = hp_[1].rel = a
                ks = slice(GK * g, GK * g + GK)
                a = tt(AA[i % 2].ap[:, ks], AA[i % 2].ap[:, ks], GA[:, ks], AD)
                a = act(AW[i % 2].ap[:, ks], AA[i % 2].ap[:, ks], gelu, a, AW[i % 2].rel if g == 0 else None)
                AA[i % 2].rel = a
                state[i, g] = tt(AW[i % 2].ap[:, ks], AW[i % 2].ap[:, ks], GT[:, i, ks], M, a)
                if n:
                    ups(*steps[n - 1])
            ups(*steps[-1])
            fence()

        csets = Cell(sem("s_cols"))
        for l in range(2):
            tiles = [0, 1, 2, 3]
            own = tiles if l == 0 else [0, 1]
            T = 128 * len(own)
            w_in = A["w_in"][l]
            tk = S.dma(csets, cols, A["cols"][l])
            tk = S.dma(csets, KE, A["keysT"][l])
            t_ht = modulate(l, A["norm1_g"][l], 0, tiles)
            pos[0] = STAGE
            Z = buf(4, 928)
            CQ = buf(2, 128)
            CK = buf(128)
            qt = buf(768)
            kt = buf(768)
            kvt = buf(1024)
            VV = buf(4, 512)
            QT = buf(8, 512)
            KT = buf(8, 512)
            PB = [Slot(qt[:, 0:512]), Slot(kt[:, 0:512])]
            PT = [Slot(buf(512)) for _ in range(2)]
            junk = PT[0].ap
            rt = PT[1].ap[:, 0:384].rearrange("p (a n) -> p a n", n=128)
            s0 = wblock(w_in, 0, 512)
            tok_major(s0, 512, lambda t: Z[:, t, 0:512], tiles, t_ht)
            s0 = wblock(w_in, 512, 416)
            tok_major(s0, 416, lambda t: Z[:, t, 512:928], own, t_ht)
            tz = (V.last(), S.last())
            sq = wload([(lambda a: a[:, 0:1536].rearrange("p (k n) -> p k n", n=768),
                         A["w_uq"][l].rearrange("(k p) n -> p k n", p=128)),
                        (lambda a: a[:, 1536:2560], A["w_ukv"][l]),
                        (lambda a: a[0:64, 2560:2816].rearrange("p (g d) -> p g d", g=4),
                         A["w_grp"][l].rearrange("g c d -> c g d"))])
            wuq = sq.ap[:, 0:1536].rearrange("p (k n) -> p k n", n=768)
            wukv = sq.ap[:, 1536:2560]
            wgrp = sq.ap[0:64, 2560:2816].rearrange("p (g d) -> p g d", g=4)
            for t in tiles:
                ns = [(0, 256, CQ, 24, 2)] if t in own else []
                ns.append((256, 128, None, 26, 1))
                for c0, w, dst, col, nk in ns:
                    z = Z[:, t, c0:c0 + w]
                    a = norm_stat(z, small[:, 8:9], w, tz, P.last(), junk=junk[:, 0:w])
                    a = ts(z, z, small[:, 8:9], None, M, None, a)
                    b = bank()
                    for k in range(nk):
                        u = tr(b.ap[:, 128 * k:128 * k + 128], z[:, 128 * k:128 * k + 128], a, b.rel)
                    for k in range(nk):
                        o_ = CQ[:, k, :] if dst is not None else CK
                        b.rel = act(o_, b.ap[:, 128 * k:128 * k + 128], ACT.Copy, u, tk, scale=cols[:, col + k:col + k + 1])
                tc = S.last()

                def rope(v, n):
                    x1, x2 = v[:, :, :, 0, :], v[:, :, :, 1, :]
                    co = krc[:, t, :, :].unsqueeze(1).to_broadcast([128, n, 2, 8])
                    si = krs[:, t, :, :].unsqueeze(1).to_broadcast([128, n, 2, 8])
                    r = [rt[:, i, 0:16 * n].rearrange("p (h a e) -> p h a e", a=2, e=8) for i in range(3)]
                    tt(r[0], x1, co, M, tok_x)
                    tt(r[1], x2, si, M)
                    tt(r[2], x1, si, M)
                    tt(x1, r[0], r[1], SU)
                    tt(r[0], x2, co, M)
                    return tt(x2, r[2], r[0], AD)

                if t in own:
                    for j in range(2):
                        b = bank()
                        for k in range(2):
                            u = mm(b.ap[:, 0:384], CQ[:, k, :], wuq[:, k, 384 * j:384 * j + 384], k == 0, k == 1, tc, sq.tok, b.rel)
                        b.rel = copy(qt[:, 384 * j:384 * j + 384], b.ap[:, 0:384], u, q=V)
                    qv = qt.rearrange("p (h c) -> p h c", c=96)
                    if t < 2:
                        rope(qv[:, :, 64:96].rearrange("p h (a s e) -> p h a s e", a=2, s=2), 8)
                    tq = V.last()
                    for j in range(2):
                        b = bank()
                        for i in range(4):
                            u = tr(b.ap[0:96, 128 * i:128 * i + 128], qv[:, 4 * j + i, :], tq, b.rel)
                        b.rel = copy(QT[0:96, 4 * j:4 * j + 4, 128 * t:128 * t + 128],
                                     b.ap[0:96, :].rearrange("p (i n) -> p i n", n=128), u, q=S)
                    V.hold(u)
                for j in range(2):
                    b = bank()
                    u = mm(b.ap, CK, wukv[:, 512 * j:512 * j + 512], True, True, tc, sq.tok, b.rel)
                    b.rel = copy(kvt[:, 512 * j:512 * j + 512], b.ap, u, q=V)
                kr = Z[:, t, 384:416]
                if t < 2:
                    rope(kr.rearrange("p (h a s e) -> p h a s e", h=1, a=2, s=2), 1)
                kv3 = kvt.rearrange("p (h c) -> p h c", c=128)
                kt3 = kt.rearrange("p (h c) -> p h c", c=96)
                V(lambda e, kt3=kt3, kv3=kv3: e.tensor_copy(kt3[:, :, 0:64], kv3[:, :, 0:64]), P.last())
                a = V(lambda e, kt3=kt3, kr=kr: e.tensor_copy(kt3[:, :, 64:96], kr.unsqueeze(1).to_broadcast([128, 8, 32])))
                V(lambda e, kv3=kv3, t=t: e.tensor_copy(VV[:, t, :].rearrange("p (h c) -> p h c", c=64), kv3[:, :, 64:128]))
                for j in range(2):
                    b = bank()
                    for i in range(4):
                        u = tr(b.ap[0:96, 128 * i:128 * i + 128], kt3[:, 4 * j + i, :], a, b.rel)
                    b.rel = copy(KT[0:96, 4 * j:4 * j + 4, 128 * t:128 * t + 128],
                                 b.ap[0:96, :].rearrange("p (i n) -> p i n", n=128), u, q=S)
                V.hold(u)
            fence()
            AT = H2[:, 0:2, :].rearrange("p a b -> p (a b)").rearrange("p (k n) -> p k n", n=512)
            FT = H2[:, 2, :].rearrange("p (k n) -> p k n", n=512)
            PL = H2[:, 3, :].rearrange("p (k n) -> p k n", n=512)
            rs, nm, mx = small[:, 16:24], small[:, 24:32], small[:, 32:40]
            ring_banks[0] = [0, 1, 2, 3, 4, 5]
            for t in own:
                k0, nk = (0, 4) if t < 2 else (2, 2)
                ab = banks[6 + t % 2]
                for h in range(8):
                    pb, pt = PB[h % 2], PT[h % 2]
                    b = bank()
                    u = mm(b.ap[:, 0:128 * nk], QT[0:96, h, 128 * t:128 * t + 128], KT[0:96, h, 128 * k0:128 * (k0 + nk)], True, True, b.rel)
                    red(mx[:, h:h + 1], b.ap[:, 0:128 * nk], ALU.max, u)
                    a = ts(nm[:, h:h + 1], mx[:, h:h + 1], -ATT_SCALE, None, M, None)
                    b.rel = a = act(pb.ap[:, 0:128 * nk], b.ap[:, 0:128 * nk], ACT.Exp, a, pb.rel, scale=ATT_SCALE, bias=nm[:, h:h + 1], accum=rs[:, h:h + 1])
                    b = bank()
                    for i in range(nk):
                        u = tr(b.ap[:, 128 * i:128 * i + 128], pb.ap[:, 128 * i:128 * i + 128], a, b.rel)
                    pb.rel = u
                    b.rel = a = copy(pt.ap[:, 0:128 * nk], b.ap[:, 0:128 * nk], u, pt.rel, q=(V, S)[h % 2])
                    for i in range(nk):
                        u = mm(ab.ap[:, 64 * h:64 * h + 64], pt.ap[:, 128 * i:128 * i + 128], VV[:, k0 + i, 64 * h:64 * h + 64], i == 0, i == nk - 1, a, ab.rel)
                    pt.rel = u
                recip(rs, rs, S.last())
                at = kvt[:, 0:512]
                ab.rel = a = tt(at.rearrange("p (h c) -> p h c", c=64), ab.ap.rearrange("p (h c) -> p h c", c=64),
                                rs.unsqueeze(2).to_broadcast([128, 8, 64]), M, u)
                b = bank()
                for i in range(4):
                    u = tr(b.ap[:, 128 * i:128 * i + 128], at[:, 128 * i:128 * i + 128], a, b.rel)
                b.rel = copy(AT[:, :, 128 * t:128 * t + 128], b.ap.rearrange("p (i n) -> p i n", n=128), u, q=S)
                V.hold(u)
            ring_banks[0] = list(range(8))
            fence()
            for who in range(len(own) // 2):
                cz = [QT[:, i, 0:512].rearrange("p (k n) -> p k n", n=256) for i in range(2)]
                for f, km in enumerate((kcos, ksin)):
                    for c in range(2):
                        b = bank()
                        for k in range(2):
                            u = mm(b.ap[:, 0:256], Z[:, 2 * who + k, 416 + 128 * c:544 + 128 * c], km[:, k, :], k == 0, k == 1, b.rel)
                        b.rel = act(cz[f][:, c, :], b.ap[:, 0:256], ACT.Copy, u, scale=1.0 if f == 0 else -1.0)
                tz = S.last()
                for c in range(2):
                    b = bank()
                    n = 0
                    for f, km in enumerate((kcos, ksin)):
                        for k in range(2):
                            u = mm(b.ap[:, 0:256], km[:, k, 128 * c:128 * c + 128], cz[f][:, k, :], n == 0, n == 3, tz, b.rel)
                            n += 1
                    b.rel = copy(FT[:, c, 256 * who:256 * who + 256], b.ap[:, 0:256], u, q=V)
                pz = QT[0:64, 4:6, :].rearrange("p a (b n) -> p (a b) n", n=256)
                for g in range(4):
                    b = bank()
                    for k in range(2):
                        u = mm(b.ap[0:64, 0:256], Z[:, 2 * who + k, 672 + 64 * g:736 + 64 * g], kpool[:, g, k, :], k == 0, k == 1, b.rel)
                    b.rel = copy(pz[:, g, :], b.ap[0:64, 0:256], u, q=S)
                tz = S.last()
                for g in range(4):
                    r = slice(64 * (g % 2), 64 * (g % 2) + 64)
                    b = bank()
                    u = mm(b.ap[r, 0:256], wgrp[:, g, :], pz[:, g, :], True, True, tz, b.rel)
                    b.rel = ts(PL[r, g // 2, 256 * who:256 * who + 256], b.ap[r, 0:256], cols[r, 27 + g // 2:28 + g // 2], None, M, None, u)
                S.hold(u)
            sq.rel = u
            fence()
            dump(f"at{l}", AT)
            dump(f"ft{l}", FT)
            dump(f"pl{l}", PL)
            MX = QT
            gs = [Z[:, i, 0:512] for i in range(3)]
            ty = KT[:, 0, :]
            for j in range(8):
                parts = [(lambda a, i=i: a[:, 1024 * i:1024 * i + 1024].rearrange("p (k n) -> p k n", n=128),
                          w_in[:, 928 + 1024 * i + 128 * j:928 + 1024 * i + 128 * j + 128].rearrange("(k p) n -> p k n", p=128))
                         for i in range(3)]
                offs = []
                o = 3072
                for name, nk in (("w_oa", 4), ("w_ob", 2), ("w_oc", 2)):
                    parts.append((lambda a, o=o, nk=nk: a[:, o:o + 128 * nk].rearrange("p (k n) -> p k n", n=128),
                                  A[name][l][:, 128 * j:128 * j + 128].rearrange("(k p) n -> p k n", p=128)))
                    offs.append((o, nk))
                    o += 128 * nk
                s = wload(parts)
                for i, src in enumerate((AT, FT, PL)):
                    b = bank()
                    wg = s.ap[:, 1024 * i:1024 * i + 1024].rearrange("p (k n) -> p k n", n=128)
                    for k in range(8):
                        u = mm(b.ap[:, 0:T], wg[:, k, :], HT[:, k, 0:T], k == 0, k == 7, s.tok, b.rel)
                    b.rel = a = act(gs[i][:, 0:T], b.ap[:, 0:T], ACT.Sigmoid, u, V.last(), bias=cols[:, 8 * i + j:8 * i + j + 1])
                    b = bank()
                    o, nk = offs[i]
                    wy = s.ap[:, o:o + 128 * nk].rearrange("p (k n) -> p k n", n=128)
                    for k in range(nk):
                        u = mm(b.ap[:, 0:T], wy[:, k, :], src[:, k, 0:T], k == 0, k == nk - 1, b.rel)
                    if i == 0:
                        b.rel = tt(MX[:, j, 0:T], gs[i][:, 0:T], b.ap[:, 0:T], M, a, u)
                    else:
                        b.rel = tt(ty[:, 0:T], gs[i][:, 0:T], b.ap[:, 0:T], M, a, u)
                        tt(MX[:, j, 0:T], MX[:, j, 0:T], ty[:, 0:T], AD)
                s.rel = u
            tmx = V.last()
            grs = [mrow(l, who, 2) for who in range(len(own) // 2)]
            for c in range(2):
                s = wblock(A["w_out"][l], 512 * c, 512)
                for t in own:
                    b = bank()
                    for k in range(8):
                        u = mm(b.ap, MX[:, k, 128 * t:128 * t + 128], s.w[:, k, :], k == 0, k == 7, s.tok, b.rel, tmx)
                    g = grs[t // 2]
                    b.rel = tt(ty, b.ap, g.ap[:, 512 * c:512 * c + 512], M, u, g.tok)
                    tt(X(t)[:, 512 * c:512 * c + 512], X(t)[:, 512 * c:512 * c + 512], ty, AD)
                    g.rel = V.last()
                s.rel = u
            fence()
            dump(f"x1_{l}", XR)
            t_ht = modulate(l, A["norm2_g"][l], 3, own)
            grs = [mrow(l, who, 5) for who in range(len(own) // 2)]
            peer(l, A["w_pq"][l], A["peer_down"], A["peer_up"], 16384 * l, own, ACT.Gelu_apprx_tanh, False, grs, STAGE, t_ht, tk)
            dump(f"x2_{l}", XR)
            if l == 0:
                dump("c2_0", CR)

        fg = brow(A["final_g"])
        for t in range(2):
            a = norm_stat(XR[:, t, :], small[:, t:t + 1], D, junk=H2[:, t, :])
            stt(XR[:, t, :], XR[:, t, :], small[:, t:t + 1], fg.ap, M, M, a, fg.tok)
        fg.rel = V.last()
        dump("xf", XR)
        t_ht = modulate(2, A["norm1_g_2"][0], 0, [0, 1])
        marks = fence()

        K2 = arena[:, BASE:BASE + sum(WIDTH[k] for k in GROUP2)]
        o = 0
        k2 = {}
        for k in GROUP2:
            k2[k] = K2[:, o:o + WIDTH[k]]
            o += WIDTH[k]
        dist = k2["dist"].rearrange("p (k n) -> p k n", n=256)
        lcnt = k2["lcnt"].rearrange("p (k n) -> p k n", n=256)
        tri = k2["tri"].rearrange("p (k n) -> p k n", n=128)
        msk = k2["msk"].rearrange("p (k n) -> p k n", n=128)
        sel = k2["sel"].rearrange("p (k n) -> p k n", n=128)
        selT = k2["selT"].rearrange("p (k n) -> p k n", n=128)
        hb = k2["hblk"].unsqueeze(2).to_broadcast([128, 8, 64])
        c2 = Cell(sem("s_const2"))
        Y.dma(c2, K2, A["k2"], marks)
        tk2 = Y.dma(c2, KE[:, 0:256], A["keysT_2"])
        pos[0] = STAGE
        Z2 = buf(2, 3328)
        p1 = pos[0]
        ZP = buf(2, 1792)
        ZN = buf(2, 1792)
        MU = buf(2, 1792)
        G(lambda e: e.memset(ZP[0:1, 0, :], 0.0))
        t0 = G(lambda e: e.memset(ZN[:, 1, :], 0.0))
        cmu, csh, crw = Cell(sem("s_mu")), Cell(sem("s_shift")), Cell(sem("s_rows"))
        Y.dma(cmu, MU[:, 0, :], A["mu_prev_2"][0].partition_broadcast(128))
        t_mu = Y.dma(cmu, MU[:, 1, :], A["mu_next_2"][0].partition_broadcast(128))
        for j in range(7):
            n = 512 if j < 6 else 256
            s = wblock(A["w_in_2"][0], 512 * j, n)
            tok_major(s, n, lambda t: Z2[:, t, 512 * j:512 * j + n], [0, 1], t_ht)
        tz = (V.last(), S.last(), t0)
        MIX = H2[:, 2:4, :]
        R = slice(1536, 3328)
        for t in range(2):
            S.dma(csh, ZP[1:128, t, :], Z2[0:127, t, R], tz)
            S.dma(csh, ZN[0:127, t, :], Z2[1:128, t, R])
        S.dma(csh, ZP[0:1, 1, :], Z2[127:128, 0, R])
        tz = S.dma(csh, ZN[127:128, 0, :], Z2[0:1, 1, R])
        for t in range(2):
            z = Z2[:, t, R]
            tt(ZP[:, t, :], ZP[:, t, :], z, SU, tz, t_mu)
            tt(ZP[:, t, :], ZP[:, t, :], MU[:, 0, :], M)
            tt(ZN[:, t, :], ZN[:, t, :], z, SU, tz, t_mu, q=G)
            a = tt(ZN[:, t, :], ZN[:, t, :], MU[:, 1, :], M, q=G)
            tt(z, z, ZP[:, t, :], AD, a)
            tt(z, z, ZN[:, t, :], AD)
        marks = fence()
        dump("zr", Z2)
        pos[0] = p1
        RW = buf(4736)
        rows = {}
        o = 0
        for name, n in (("lnx_g_2", 512), ("lnx_b_2", 512), ("k_k_2", 512), ("k_a_2", 512), ("r_k_2", 512),
                        ("w_decay0_2", 1024), ("a_gate0_2", 1024), ("q_norm_g_2", 64), ("k_norm_g_2", 64)):
            src = A[name][0]
            if name == "r_k_2":
                src = src.rearrange("h n -> (h n)")
            elif n == 1024:
                src = src.rearrange("a n -> (a n)")
            rows[name] = RW[:, o:o + n]
            t_rw = Y.dma(crw, rows[name], src.partition_broadcast(128), marks)
            o += n
        p2 = pos[0]
        bc0 = STAGE - 4096
        LW = arena[:, bc0:bc0 + 2560].rearrange("p (a n) -> p a n", n=512)
        for d in range(2):
            Y.dma(crw, LW[0:64, d, :], A["w_decay_up_2"][0, d], marks)
            Y.dma(crw, LW[0:64, 2 + d, :], A["a_gate_up_2"][0, d])
        t_rw = Y.dma(crw, LW[:, 4, :], A["g_up_2"][0])
        QN, KN = buf(512), buf(512)
        BI = buf(2, 256)
        PB = [Slot(buf(256)) for _ in range(2)]
        PT = [Slot(buf(256)) for _ in range(2)]
        ss, mx, nm, rs = small[:, 0:8], small[:, 8:16], small[:, 16:24], small[:, 24:32]
        QT2 = HT[:, 0:4, :].rearrange("p a b -> p (a b)").rearrange("p (h n) -> p h n", n=256)
        KT2 = HT[:, 4:8, :].rearrange("p a b -> p (a b)").rearrange("p (h n) -> p h n", n=256)
        for t in range(2):
            for c0, dst, g, tr_ in ((0, QN, "q_norm_g_2", QT2), (512, KN, "k_norm_g_2", KT2)):
                z = Z2[:, t, c0:c0 + 512]
                d3 = dst.rearrange("p (h n) -> p h n", n=64)
                tt(dst, z, z, M, t_rw)
                red(ss, d3, AD)
                a = ts(ss, ss, 1.0 / 64, 1e-6, M, AD)
                a = act(ss, ss, ACT.Sqrt, a)
                recip(ss, ss, a)
                tt(d3, z.rearrange("p (h n) -> p h n", n=64), ss.unsqueeze(2).to_broadcast([128, 8, 64]), M)
                a = tt(d3, d3, rows[g].unsqueeze(1).to_broadcast([128, 8, 64]), M)
                for j in range(2):
                    b = bank()
                    for i in range(4):
                        h = 4 * j + i
                        u = tr(b.ap[0:64, 128 * i:128 * i + 128], dst[:, 64 * h:64 * h + 64], a, b.rel)
                    b.rel = copy(tr_[0:64, 4 * j:4 * j + 4, 128 * t:128 * t + 128],
                                 b.ap[0:64, :].rearrange("p (i n) -> p i n", n=128), u, q=S)
                V.hold(u)
        tq = S.last()
        ring_banks[0] = [0, 1, 2, 3, 4, 5]
        for t in range(2):
            ab = banks[6 + t]
            for h in range(8):
                pb, pt = PB[h % 2], PT[h % 2]
                b = bank()
                u = mm(b.ap[:, 0:256], QT2[0:64, h, 128 * t:128 * t + 128], KT2[0:64, h, :], True, True, tq, b.rel)
                bi = BI[:, h % 2, :]
                stt(bi, dist[:, t, :], 2.0 ** -(h + 1), lcnt[:, t, :], M, AD, tk2)
                stt(bi, b.ap[:, 0:256], 0.125, bi, M, AD, u)
                b.rel = red(mx[:, h:h + 1], bi, ALU.max)
                a = ts(nm[:, h:h + 1], mx[:, h:h + 1], -1.0, None, M, None)
                a = act(pb.ap, bi, ACT.Exp, a, pb.rel, bias=nm[:, h:h + 1], accum=rs[:, h:h + 1])
                b = bank()
                for i in range(2):
                    u = tr(b.ap[:, 128 * i:128 * i + 128], pb.ap[:, 128 * i:128 * i + 128], a, b.rel)
                pb.rel = u
                b.rel = a = copy(pt.ap, b.ap[:, 0:256], u, pt.rel, q=S)
                for i in range(2):
                    u = mm(ab.ap[:, 64 * h:64 * h + 64], pt.ap[:, 128 * i:128 * i + 128],
                           Z2[:, i, 1024 + 64 * h:1088 + 64 * h], i == 0, i == 1, a)
                pt.rel = u
                V.hold(S.last())
            recip(rs, rs, S.last())
            ab.rel = tt(MIX[:, t, 0:512].rearrange("p (h c) -> p h c", c=64), ab.ap.rearrange("p (h c) -> p h c", c=64),
                        rs.unsqueeze(2).to_broadcast([128, 8, 64]), M, u)
            S.hold(ab.rel)
        ring_banks[0] = list(range(8))
        fence()
        pos[0] = p2
        wr = [arena[:, WR + 2048 * i:WR + 2048 * i + 2048] for i in range(6)]
        AL, BE, KA, RO, PI = [w.rearrange("p (c h s) -> p c h s", c=16, h=8) for w in wr[:5]]
        GG = wr[5][:, 0:1024].rearrange("p (t n) -> p t n", n=512)
        BON = wr[5][:, 1024:2048].rearrange("p (t n) -> p t n", n=512)
        LT = buf(256)
        LTT = buf(3, 128)
        E_ = [buf(512) for _ in range(2)]
        A_ = [buf(512) for _ in range(2)]
        KKA = [buf(512) for _ in range(2)]
        KD = [buf(512) for _ in range(2)]
        KK = buf(512)
        T1 = arena[:, bc0 + 2560:bc0 + 3072]
        T2 = arena[:, bc0 + 3072:bc0 + 3584]
        s8, s8b = small[:, 0:8], small[:, 8:16]
        CE = math.exp(-0.5)

        def h3(a):
            return a.rearrange("p (h n) -> p h n", n=64)

        def b8(a):
            return a.unsqueeze(2).to_broadcast([128, 8, 64])

        for t in range(2):
            r_, k_, v_ = (Z2[:, t, 1536 + 512 * i:2048 + 512 * i] for i in range(3))
            act(LT[:, 0:64], Z2[:, t, 3072:3136], ACT.Tanh)
            copy(LT[:, 64:128], Z2[:, t, 3136:3200], q=S)
            a = act(LT[:, 128:256], Z2[:, t, 3200:3328], ACT.Sigmoid)
            b = bank()
            tr(b.ap[0:64, 0:128], LT[:, 0:64], a, b.rel)
            tr(b.ap[0:64, 128:256], LT[:, 64:128])
            u = tr(b.ap[:, 256:384], LT[:, 128:256])
            copy(LTT[0:64, 0:2, :], b.ap[0:64, 0:256].rearrange("p (a n) -> p a n", n=128), u, q=S)
            b.rel = a = copy(LTT[:, 2, :], b.ap[:, 256:384], q=S)
            b = bank()
            u = mm(b.ap, LTT[:, 2, :], LW[:, 4, :], True, True, a, b.rel)
            b.rel = copy(GG[:, t, :], b.ap, u, q=S)
            ts_ = []
            for d in range(2):
                b = bank()
                u = mm(b.ap, LTT[0:64, 0, :], LW[0:64, d, :], True, True, b.rel)
                b.rel = x = tt(E_[d], b.ap, rows["w_decay0_2"][:, 512 * d:512 * d + 512], AD, u)
                act(E_[d], E_[d], ACT.Sigmoid, x)
                b = bank()
                u = mm(b.ap, LTT[0:64, 1, :], LW[0:64, 2 + d, :], True, True, b.rel)
                b.rel = x = tt(A_[d], b.ap, rows["a_gate0_2"][:, 512 * d:512 * d + 512], AD, u)
                ta = act(A_[d], A_[d], ACT.Sigmoid, x)
            tt(KK, k_, rows["k_k_2"], M)
            tt(T1, KK, KK, M)
            red(s8, h3(T1), AD)
            a = ts(s8, s8, 1e-12, None, ALU.max, None)
            a = act(s8, s8, ACT.Sqrt, a)
            recip(s8, s8, a)
            tt(h3(KK), h3(KK), b8(s8), M)
            for d in range(2):
                tt(KKA[d], KK, A_[d], M, ta)
                stt(KD[d], A_[d], -1.0, rows["k_a_2"], AD, M)
                tkk = stt(KD[d], KD[d], 1.0, k_, AD, M)
            tt(T1, A_[0], A_[1], AD)
            ts(T1, T1, 0.5, -1.0, M, AD)
            tt(T1, T1, rows["k_a_2"], M)
            stt(T1, T1, 1.0, k_, AD, M)
            tt(T1, T1, r_, M)
            tt(T1, T1, rows["r_k_2"], M)
            red(s8b, h3(T1), AD)
            tt(h3(BON[:, t, :]), h3(v_), b8(s8b), M)
            for hf in range(2):
                def cum(i0):
                    b = bank()
                    for d in range(2):
                        for i in range(4):
                            h = 4 * hf + i
                            u = mm(b.ap[64 * d:64 * d + 64, 128 * i:128 * i + 128], E_[d][:, 64 * h:64 * h + 64],
                                   tri[:, i0 + d, :], True, True, ta, b.rel)
                    return b, u

                def turned(srcs):
                    b = bank()
                    for d in range(2):
                        for i in range(4):
                            h = 4 * hf + i
                            u = mm(b.ap[64 * d:64 * d + 64, 128 * i:128 * i + 128], srcs[d][:, 64 * h:64 * h + 64],
                                   ident, True, True, tkk, b.rel)
                    return b, u

                def at4(w):
                    return w[:, 8 * t:8 * t + 8, 4 * hf:4 * hf + 4, :].rearrange("p c h s -> p h c s")

                def v4(a):
                    return a.rearrange("p (h c s) -> p h c s", h=4, c=8)

                S.hold(V.last())
                b, u = cum(0)
                act(at4(PI), v4(b.ap), ACT.Exp, u, scale=-CE)
                b.rel = act(T1, b.ap, ACT.Exp, scale=CE)
                b, u = cum(2)
                b.rel = x = act(T2, b.ap, ACT.Exp, u, scale=-CE)
                for srcs, dst, f in (((KK, KK), AL, v4(T2)), (KKA, BE, v4(T1)), (KD, KA, v4(T1)),
                                     ((r_, r_), RO, at4(PI))):
                    b, u = turned(srcs)
                    b.rel = tt(at4(dst), f, v4(b.ap), M, u, x)
            S.hold(V.last(), P.last())
            V.hold(P.last())
        fence()
        dump("al", wr[0])
        dump("be", wr[1])
        pos[0] = p1 + 1024
        TMP = [HT[:, i, :] for i in range(8)]
        LK = buf(4, 128)
        AR = buf(4, 64)
        TA = buf(4, 128)
        PD = []
        for d in range(2):
            PD.append(dict(rb=buf(4, 128), rk=buf(4, 128), tl=buf(4, 128), br=buf(4, 64), kr=buf(4, 64), ve=buf(4, 512)))
        ST = arena[:, bc0:bc0 + 512]
        UE = [arena[:, bc0 + 512 * (1 + d):bc0 + 512 * (2 + d)] for d in range(2)]
        YE = [arena[:, bc0 + 512 * (3 + d):bc0 + 512 * (4 + d)] for d in range(2)]
        memset(V, ST, 0.0)
        ring_banks[0] = [0, 1, 2, 3, 4, 5]
        left = {0: 16, 1: 16}

        def prep(d, chunks):
            q = PD[d]
            pr = slice(64 * d, 64 * d + 64)

            def four(f, *after):
                b = bank()
                for n, c in enumerate(chunks):
                    u = f(b.ap, n, c, after, b.rel)
                return b, u

            def pair(l, r, mi, dst, *after):
                b, u = four(lambda o_, n, c, *w: mm(o_[:, 128 * n:128 * n + 128], l[pr, c, :, :].rearrange("p h s -> p (h s)"),
                                                   r[pr, c, :, :].rearrange("p h s -> p (h s)"), True, True, *w), *after)
                b.rel = tt(dst, b.ap.rearrange("p (n i) -> p n i", i=128), msk[:, mi, :].unsqueeze(1).to_broadcast([128, 4, 128]), M, u)
                return b.rel

            def v(a):
                return a.rearrange("p (n i) -> p n i", i=128)

            L, Mt, L2, M2, L4, M4, L8, Q = [v(a) for a in TMP]
            pair(AL, BE, d, L)
            tm = pair(BE, AL, 1 - d, Mt)
            pair(AL, KA, d, LK)
            pair(BE, RO, 3 - d, q["rb"])
            pair(KA, RO, 3 - d, q["rk"])
            idn = ident[pr, 64 * d:64 * d + 64]
            for src, dst in ((AL, AR), (BE, q["br"]), (KA, q["kr"])):
                b, u = four(lambda o_, n, c, *w: mm(o_[:, 64 * n:64 * n + 64], src[pr, c, :, :].rearrange("p h s -> p (h s)"), idn, True, True, *w))
                b.rel = copy(dst, b.ap[:, 0:256].rearrange("p (n i) -> p n i", i=64), u, q=S)
            idb = ident.unsqueeze(1).to_broadcast([128, 4, 128])
            tQ = tt(Q, idb, Mt, SU)

            def prod(l, r, *after):
                return four(lambda o_, n, c, *w: mm(o_[:, 128 * n:128 * n + 128], l[:, n, :], r[:, n, :], True, True, *w), *after)

            def power(l, r, dst, *after):
                b, u = prod(l, r, *after)
                b.rel = copy(dst, v(b.ap), u, q=S)
                return b.rel

            x = power(Mt, L, L2, tQ)
            x = power(L, Mt, M2, tQ)
            power(M2, L2, L4, x)
            y = power(L2, M2, M4, x)
            z = power(M4, L4, L8, y)
            for l, w in ((L2, x), (L4, y), (L8, z)):
                b, u = prod(l, Q, w, tQ)
                b.rel = tQ = tt(Q, Q, v(b.ap), AD, u)
            b, u = four(lambda o_, n, c, *w: mm(o_[pr, 128 * n:128 * n + 128], AR[:, n, :], Q[:, n, :], True, True, *w), tQ)
            b.rel = copy(TA[pr, :, :], v(b.ap[pr, :]), u, q=S)
            b, u = prod(LK, Q, tQ)
            b.rel = copy(q["tl"], v(b.ap), u, q=S)
            V.hold(u)
            for n, c in enumerate(chunks):
                b = bank()
                u = mm(b.ap, selT[:, c % 8, :], Z2[:, c // 8, 2560:3072], True, True, b.rel)
                b.rel = tt(h3(q["ve"][:, n, :]), h3(b.ap), hb, M, u)

        def step(d, n, c):
            q = PD[d]
            pr = slice(64 * d, 64 * d + 64)
            b = bank()
            mm(b.ap, TA[pr, n, :], ST[pr, :], True, False, V.last(), S.last(), b.rel)
            u = mm(b.ap, q["tl"][:, n, :], q["ve"][:, n, :], False, True)
            b.rel = x = stt(h3(UE[d]), h3(b.ap), -1.0, hb, M, M, u)
            b = bank()
            mm(b.ap[pr, :], q["br"][:, n, :], UE[d], True, False, x, b.rel)
            us = mm(b.ap[pr, :], q["kr"][:, n, :], q["ve"][:, n, :], False, True)
            b3 = bank()
            mm(b3.ap, RO[pr, c, :, :].rearrange("p h s -> p (h s)"), ST[pr, :], True, False, b3.rel)
            mm(b3.ap, q["rb"][:, n, :], UE[d], False, False)
            u = mm(b3.ap, q["rk"][:, n, :], q["ve"][:, n, :], False, True)
            b.rel = tt(ST[pr, :], ST[pr, :], b.ap[pr, :], AD, u)
            pc = PI[pr, c, :, 15 if d == 0 else 0]
            tt(h3(ST[pr, :]), h3(ST[pr, :]), pc.unsqueeze(2).to_broadcast([64, 8, 64]), M)
            b3.rel = x = tt(h3(YE[d]), h3(b3.ap), hb, M, u)
            ti = c // 8
            left[ti] -= 1
            u = mm(banks[6 + ti].ap, sel[:, c % 8, :], YE[d], left[ti] == 15, left[ti] == 0, x, banks[6 + ti].rel)
            V.hold(u)

        for bt in range(4):
            ch = [[4 * bt + n for n in range(4)], [15 - 4 * bt - n for n in range(4)]]
            for d in range(2):
                prep(d, ch[d])
                fence()
            for n in range(4):
                for d in range(2):
                    step(d, n, ch[d][n])
            fence()
        for t in range(2):
            yb = banks[6 + t]
            y3 = h3(yb.ap)
            red(s8, y3, AD, P.last())
            ts(s8, s8, 1.0 / 64, None, M, None)
            yb.rel = tt(h3(T2), y3, b8(s8), SU)
            tt(UE[0], T2, T2, M)
            red(s8, h3(UE[0]), AD)
            a = ts(s8, s8, 1.0 / 64, 64e-5, M, AD)
            a = act(s8, s8, ACT.Sqrt, a)
            recip(s8, s8, a)
            tt(h3(T2), h3(T2), b8(s8), M)
            tt(T2, T2, rows["lnx_g_2"], M)
            tt(T2, T2, rows["lnx_b_2"], AD)
            tt(T2, T2, BON[:, t, :], AD)
            a = tt(MIX[:, t, 512:1024], T2, GG[:, t, :], M)
            for j in range(2):
                b = bank()
                for i in range(4):
                    u = tr(b.ap[:, 128 * i:128 * i + 128], MIX[:, t, 512 * j + 128 * i:512 * j + 128 * i + 128], a, b.rel)
                b.rel = copy(HT[:, 4 * j:4 * j + 4, 128 * t:128 * t + 128], b.ap.rearrange("p (i n) -> p i n", n=128), u, q=S)
        ring_banks[0] = list(range(8))
        marks = fence()
        dump("mix", MIX)
        for s in wslots + bcs:
            s.rel = marks
        gr = mrow(2, 0, 2)
        pos[0] = STAGE
        ty = buf(512)
        tz = S.last()
        for c in range(2):
            s = wblock(A["w_out_2"][0], 512 * c, 512)
            for t in range(2):
                b = bank()
                for k in range(8):
                    u = mm(b.ap, HT[:, k, 128 * t:128 * t + 128], s.w[:, k, :], k == 0, k == 7, s.tok, b.rel, tz)
                b.rel = tt(ty, b.ap, gr.ap[:, 512 * c:512 * c + 512], M, u, gr.tok)
                tt(X(t)[:, 512 * c:512 * c + 512], X(t)[:, 512 * c:512 * c + 512], ty, AD)
            s.rel = u
        gr.rel = V.last()
        fence()
        dump("x3", XR)
        t_ht = modulate(2, A["norm2_g_2"][0], 3, [0, 1])
        peer(2, A["peer_w_query_2"][0], A["peer_u_2"], A["peer_v_2"], 0, [0, 1], ACT.Gelu, True,
             [mrow(2, 0, 5)], STAGE, t_ht, tk2)
        for t in range(2):
            Y.dma(cout, out[0, 128 * t:128 * t + 128, :], XR[:, t, :], V.last())

        bodies = ((V, "vector"), (S, "scalar"), (P, "tensor"), (G, "gpsimd"), (Y, "sync"))
        block = ctx.enter_context(nc.Block())

        @block.vector
        def _(eng):
            V.play(eng)

        @block.scalar
        def _(eng):
            S.play(eng)

        @block.tensor
        def _(eng):
            P.play(eng)

        @block.gpsimd
        def _(eng):
            G.play(eng)

        @block.sync
        def _(eng):
            Y.play(eng)
            for c in (cout, csm[2], csm[3], cdbg):
                if c is not None and c.n:
                    eng.wait_ge(c.sem, c.n)


_NAMES = ["x", "ctx", "w_mod", "b_mod", "norm1_g", "norm2_g", "w_in", "w_uq", "w_ukv", "w_oa", "w_ob", "w_grp",
          "w_oc", "w_out", "w_pq", "final_g", "ada_w_2", "ada_b_2", "norm1_g_2", "w_in_2", "mu_prev_2",
          "mu_next_2", "q_norm_g_2", "k_norm_g_2", "w_decay0_2", "w_decay_up_2", "a_gate0_2", "a_gate_up_2",
          "g_up_2", "k_k_2", "k_a_2", "r_k_2", "lnx_g_2", "lnx_b_2", "w_out_2", "norm2_g_2", "peer_w_query_2"]


def layout(inputs):
    f = {k: np.ascontiguousarray(inputs[k]) for k in _NAMES}
    f["peer_down"] = np.asarray(inputs["peer_down"]).reshape(2 * 16384, D)
    f["peer_up"] = np.asarray(inputs["peer_up"]).reshape(2 * 16384, D)
    f["peer_u_2"] = np.asarray(inputs["peer_u_2"]).reshape(16384, D)
    f["peer_v_2"] = np.asarray(inputs["peer_v_2"]).reshape(16384, D)
    vecs = [np.asarray(inputs[k]).reshape(128, 8) for k in ("c", "c_ctx", "c_2")]
    f["cvec"] = np.ascontiguousarray(np.stack(vecs, -1).reshape(128, 24))
    f["cols"] = np.ascontiguousarray(np.concatenate(
        [np.asarray(inputs[k]).reshape(2, n, 128).transpose(0, 2, 1)
         for k, n in (("b_gate", 24), ("q_norm_g", 2), ("kv_norm_g", 1), ("pool_scale", 2))], 2))
    f["keysT"] = np.ascontiguousarray(np.asarray(inputs["peer_keys"]).transpose(0, 4, 1, 2, 3).reshape(2, 128, 2048))
    f["keysT_2"] = np.ascontiguousarray(np.concatenate(
        [np.asarray(inputs["peer_sub_keys1_2"])[0].T, np.asarray(inputs["peer_sub_keys2_2"])[0].T], 1))
    c = const_tables()
    for name, group in (("k0", GROUP0), ("k1", GROUP1), ("k2", GROUP2)):
        f[name] = np.ascontiguousarray(np.concatenate([c[k] for k in group], 1))
    return f


def build(nc, arrays, debug=None):
    A = {k: nc.dram_tensor("in_" + k, a.shape, mybir.dt.from_np(a.dtype), kind="ExternalInput").ap()
         for k, a in arrays.items()}
    out = nc.dram_tensor("out_x", (1, 256, D), F32, kind="ExternalOutput").ap()
    dbg = None
    if debug:
        dbg = {k: nc.dram_tensor("dbg_" + k, s, F32, kind="ExternalOutput").ap() for k, s in debug.items()}
    program(nc, A, out, dbg)


def kernel(**inputs):
    import concourse.bacc as bacc
    from concourse.bass_utils import run_bass_kernel_spmd

    arrays = layout(inputs)
    nc = bacc.Bacc("TRN2", target_bir_lowering=False, num_devices=1)
    build(nc, arrays)
    r = run_bass_kernel_spmd(nc, [{"in_" + k: a for k, a in arrays.items()}], core_ids=[0])
    return r.results[0]["out_x"]
```

```python
import math
import numpy as np
import concourse.bass as bass
import concourse.mybir as mybir
from contextlib import ExitStack

F32 = mybir.dt.float32
U32 = mybir.dt.uint32
I32 = mybir.dt.int32
FAST, SLOW = 0.8, -1.0
RATES = [0.95, 0.5, 0.4, 0.6, 4.0, 0.8, 2.0, 0.45]
ALU = mybir.AluOpType
ACT = mybir.ActivationFunctionType
AX = mybir.AxisListType.X

D = 1024
NEG = -3.0e38
ATT_SCALE = 96 ** -0.5
WINDOWS = (2, 4, 8, 16)
PATTERNS = ((128, 1), (512, 4), (2048, 16))


def const_tables():
    t = np.arange(256)
    i = np.arange(128)
    c = {}
    c["ident"] = np.eye(128)
    c["iota"] = np.tile(np.arange(16.0), (128, 1))

    def halves(m):
        return m.reshape(2, 128, -1).transpose(1, 0, 2)

    a = 2.0 * np.pi * ((t[:, None] * t[None, :]) % 256) / 256.0
    c["cos"] = halves(np.cos(a) / 16.0)
    c["sin"] = halves(np.sin(a) / 16.0)
    pool = np.zeros((4, 256, 256))
    for g, w in enumerate(WINDOWS):
        lo, hi = np.clip(t - w // 2, 0, 256), np.clip(t - w // 2 + w, 0, 256)
        for u in range(256):
            pool[g, lo[u]:hi[u], u] = 1.0 / (hi[u] - lo[u])
        pool[g] -= np.eye(256)
    c["pool"] = np.stack([halves(p) for p in pool], 1)
    freq = np.float32(10000.0) ** (-np.arange(0, 16, 2, dtype=np.float32) / np.float32(16))
    ang = np.stack([(t // 64)[:, None] * freq, (t % 64)[:, None] * freq], 1).astype(np.float32)
    c["rcos"] = np.cos(ang).reshape(2, 128, 16).transpose(1, 0, 2)
    c["rsin"] = np.sin(ang).reshape(2, 128, 16).transpose(1, 0, 2)
    d = np.abs(t[:, None] - t[None, :])
    n = np.zeros((256, 256))
    for w, dil in PATTERNS:
        n += (d % dil == 0) & (d // dil <= w // (2 * dil))
    c["dist"] = halves(-d.astype(np.float64))
    c["lcnt"] = halves(np.where(n > 0, np.log(np.maximum(n, 1)), -1e30))
    blk = (i[:, None] // 32) == (i[None, :] // 32)
    b16 = (i[:, None] // 16) == (i[None, :] // 16)
    le, lt = i[:, None] <= i[None, :], i[:, None] < i[None, :]
    c["tri"] = np.stack([blk & le, blk & le.T, blk & lt, blk & lt.T], 1)
    c["msk"] = np.stack([b16 & lt.T, b16 & lt, blk & le.T, blk & le, blk & ~b16 & lt.T, blk & ~b16 & lt,
                         blk & lt.T, blk & lt], 1)
    h, s = i // 32, i % 32
    sel = np.zeros((4, 128, 128))
    for q in range(4):
        sel[q, i, 32 * q + s] = 1.0
    c["sel"] = sel.transpose(1, 0, 2)
    c["selT"] = sel.transpose(2, 0, 1)
    c["hblk"] = np.concatenate([h[:, None] == np.arange(4)[None, :]] * 2, 1) * np.array([1.0] * 4 + [-1.0] * 4)
    return {k: np.ascontiguousarray(v.reshape(128, -1), dtype=np.float32) for k, v in c.items()}


GROUP0 = ("ident", "iota")
GROUP1 = ("cos", "sin", "pool", "rcos", "rsin")
GROUP2 = ("dist", "lcnt", "tri", "msk", "sel", "selT", "hblk")
WIDTH = {"ident": 128, "iota": 16, "cos": 512, "sin": 512, "pool": 2048, "rcos": 32, "rsin": 32,
         "dist": 512, "lcnt": 512, "tri": 512, "msk": 1024, "sel": 512, "selT": 512, "hblk": 8}


class Job:

    def __init__(self, slots=None):
        self.last, self.held, self.slots, self.turn = {}, {}, slots, 0


class Queue:

    def __init__(self, sem, chained, jobs):
        self.sem, self.items, self.n, self.chained, self.jobs = sem, [], 0, chained, jobs
        self.cost = 0.0

    def last(self):
        return self.jobs[-1].last.get(self, (self.sem, 0))

    def hold(self, *tokens):
        held = self.jobs[-1].held
        held[self] = held.get(self, ()) + tokens

    def __call__(self, fn, *after, free=False, cost=0.0):
        own = (self.last(),) if self.chained and not free else ()
        self.items.append(((after, own, self.jobs[-1].held.pop(self, ())), fn, self.sem, 1))
        self.n += 1
        self.cost += cost
        self.jobs[-1].last[self] = (self.sem, self.n)
        return (self.sem, self.n)

    def dma(self, cell, out, in_, *after, **kw):
        held = self.jobs[-1].held.pop(self, ())
        self.items.append(((after, held), lambda e: e.dma_start(out, in_, **kw), cell.sem, 16))
        cell.n += 16
        return (cell.sem, cell.n)

    def gather(self, cell, out, table, idx, *after):
        held = self.jobs[-1].held.pop(self, ())
        self.items.append(((after, held), lambda e: e.indirect_dma_start(
            out=out, out_offset=None, in_=table,
            in_offset=bass.IndirectOffsetOnAxis(ap=idx, axis=0)), cell.sem, 16))
        cell.n += 16
        return (cell.sem, cell.n)

    def play(self, eng):
        seen = {}

        def wait(t):
            if not t:
                return
            if isinstance(t[0], (tuple, list)) or t[0] is None:
                for u in t:
                    if u is not None:
                        wait(u)
                return
            sem, v = t
            if v and seen.get(id(sem), 0) < v:
                eng.wait_ge(sem, v)
                seen[id(sem)] = v

        for after, fn, sem, inc in self.items:
            wait(after)
            fn(eng).then_inc(sem, inc)


class Cell:

    def __init__(self, sem):
        self.sem, self.n = sem, 0


class Slot:

    def __init__(self, ap, cell=None):
        self.ap, self.cell, self.rel = ap, cell, ()


def program(nc, A, out, dbg):
    ctx = ExitStack()
    with ctx:
        def sem(name):
            return ctx.enter_context(nc.semaphore(name))

        jobs = [Job()]
        V = Queue(sem("s_vector"), True, jobs)
        S = Queue(sem("s_scalar"), True, jobs)
        P = Queue(sem("s_tensor"), False, jobs)
        G = Queue(sem("s_gpsimd"), True, jobs)
        Y = Queue(sem("s_sync"), False, jobs)
        ENG = (V, S, P, G)

        def fence():
            marks = tuple(q.last() for q in ENG)
            for q in ENG:
                q.hold(*marks)
            return marks

        def everything():
            return tuple((q.sem, q.n) for q in ENG)

        def run(gen):
            for _ in gen:
                pass

        def together(front, back, rate, fs=None, bs=None):
            marks = everything()
            fj, bj = Job(fs), Job(bs)
            for j in (fj, bj):
                for q in ENG:
                    j.held[q] = marks + jobs[-1].held.get(q, ())
            saved = ring_banks[0]
            done, owed, now = False, 0.0, rate

            def step(j, g, ring):
                jobs.append(j)
                ring_banks[0] = ring
                try:
                    return next(g), False
                except StopIteration:
                    return None, True
                finally:
                    ring_banks[0] = saved
                    jobs.pop()

            back_done = back is None
            while not done:
                asked, done = step(fj, front, FRONT[0])
                owed += 1000.0 if done else now
                while not back_done and (owed > 0 or asked == "more"):
                    c0 = P.cost + V.cost
                    said, back_done = step(bj, back, BACK[0])
                    now = said and (said if said > 0 else rate) or now
                    owed -= P.cost + V.cost - c0
                    asked = None
                if back_done:
                    owed = 0.0
                    assert asked != "more"
            while not back_done:
                _, back_done = step(bj, back, BACK[0])
            marks = everything()
            for q in ENG:
                q.hold(*marks, *fj.held.get(q, ()), *bj.held.get(q, ()))
            return marks

        NB = 53200
        arena = ctx.enter_context(nc.sbuf_tensor("arena", [128, NB], F32))

        class Mem:

            def __init__(self, *ranges):
                self.free = [list(r) for r in ranges]

            def __call__(self, *shape, dt=F32):
                n = int(np.prod(shape))
                for r in self.free:
                    if r[1] - r[0] >= n:
                        a0 = r[0]
                        r[0] += n
                        break
                else:
                    raise ValueError(f"no room for {shape}: {self.free}")
                a = arena[:, a0:a0 + n]
                if dt is not F32:
                    a = a.bitcast(dt)
                if len(shape) == 2:
                    a = a.rearrange("p (a b) -> p a b", b=shape[1])
                elif len(shape) == 3:
                    a = a.rearrange("p (a b c) -> p a b c", b=shape[1], c=shape[2])
                elif len(shape) == 4:
                    a = a.rearrange("p (a b c d) -> p a b c d", b=shape[1], c=shape[2], d=shape[3])
                return a

        psum = ctx.enter_context(nc.psum_tensor("ps", [128, 4096], F32))
        banks = [Slot(psum[:, 512 * i:512 * i + 512]) for i in range(8)]
        turn = [0]
        ring_banks = [list(range(8))]
        FRONT, BACK = [[0, 1, 2, 3]], [[4, 5, 6, 7]]

        def bank():
            r = ring_banks[0]
            turn[0] += 1
            return banks[r[turn[0] % len(r)]]

        def size(a):
            return int(np.prod(a.shape[1:]))

        def mm(o, l, r, start, stop, *after):
            return P(lambda e: e.matmul(o, l, r, start=start, stop=stop), *after, cost=size(r) / 600)

        def tr(o, i, *after):
            return P(lambda e: e.transpose(o, i, ident), *after, cost=0.06)

        def tt(o, a, b, op, *after, q=None, **kw):
            return (q or V)(lambda e: e.tensor_tensor(o, a, b, op), *after, cost=size(o) / 900, **kw)

        def ts(o, a, s1, s2, op0, op1, *after, q=None, **kw):
            if s2 is None:
                return (q or V)(lambda e: e.tensor_scalar(o, a, s1, None, op0), *after, cost=0.1, **kw)
            return (q or V)(lambda e: e.tensor_scalar(o, a, s1, s2, op0, op1), *after, cost=0.1, **kw)

        def stt(o, a, s, b, op0, op1, *after, accum=None, **kw):
            return V(lambda e: e.scalar_tensor_tensor(o, a, s, b, op0, op1, accum_out=accum), *after, cost=size(o) / 900, **kw)

        def act(o, i, f, *after, scale=1.0, bias=0.0, accum=None, **kw):
            return S(lambda e: e.activation(o, i, f, bias=bias, scale=scale, accum_out=accum), *after, **kw)

        def copy(o, i, *after, q=None):
            if q is V:
                return V(lambda e: e.tensor_copy(o, i), *after)
            return act(o, i, ACT.Copy, *after)

        def red(o, i, op, *after):
            return V(lambda e: e.tensor_reduce(o, i, AX, op), *after)

        def recip(o, i, *after):
            return V(lambda e: e.reciprocal(o, i), *after)

        def memset(q, o, v, *after):
            return q(lambda e: e.memset(o, v), *after)

        M, AD, SU = ALU.mult, ALU.add, ALU.subtract

        keep = Mem((0, NB))
        XR, CR = keep(2, D), keep(2, D)
        K0 = keep(144)
        ident, iota = K0[:, 0:128], K0[:, 128:144]
        small = keep(64)
        cv = keep(8, 3)
        svb = keep(8, 3)
        cols2 = keep(2, 29)
        KE = keep(2048)
        KCR = keep.free[0][0]
        keep(4104)
        WR = keep.free[0][0]
        wslots = [Slot(keep(4096), Cell(sem(f"s_w{i}"))) for i in range(2)]
        BCR = keep.free[0][0]
        bcs = [Slot(keep(D), Cell(sem(f"s_bc{i}"))) for i in range(4)]
        H2R = keep.free[0][0]
        H2 = keep(4, D)
        EI = keep(4, 128, dt=I32)
        GT = keep(4, 128)
        GR = keep.free[0][0]
        BG = GR + 9728
        wslots.append(Slot(Mem((GR, BG))(4096), Cell(sem("s_w2"))))
        GR2 = GR + 4096
        wuse = [3]

        def wload(parts, *after):
            j = jobs[-1]
            slots = j.slots or list(range(wuse[0]))
            s = wslots[slots[j.turn % len(slots)]]
            j.turn += 1
            for f, src in parts:
                t = Y.dma(s.cell, f(s.ap), src, s.rel, after)
            s.tok = t
            return s

        def wblock(src, c0, n):
            v = src[:, c0:c0 + n].rearrange("(k p) n -> p k n", p=128)
            s = wload([(lambda a: a[:, 0:8 * n].rearrange("p (k n) -> p k n", n=n), v)])
            s.w = s.ap[:, 0:8 * n].rearrange("p (k n) -> p k n", n=n)
            return s

        cell0 = Cell(sem("s_const"))
        cout = Cell(sem("s_out"))
        cdbg = Cell(sem("s_dbg")) if dbg is not None else None

        def dump(name, ap):
            if dbg is None or name not in dbg:
                return
            fence()
            t = Y.dma(cdbg, dbg[name], ap, everything(), (cdbg.sem, cdbg.n))
            for q in ENG:
                q.hold(t)

        cx = Cell(sem("s_x"))
        Y.dma(cell0, K0, A["k0"])
        t_cv = Y.dma(cell0, cv, A["cvec"].rearrange("p (k n) -> p k n", n=3))
        for q in ENG:
            q.hold(t_cv)
        KC = arena[:, KCR:KCR + sum(WIDTH[k] for k in GROUP1)]
        for t in range(2):
            S.dma(cx, XR[:, t, :], A["x"][0, 128 * t:128 * t + 128, :])
            S.dma(cx, CR[:, t, :], A["ctx"][0, 128 * t:128 * t + 128, :])
        S.dma(cx, cols2, A["cols"].rearrange("l p n -> p l n"))
        S.dma(cx, KC, A["k1"])
        tok_x = S.dma(cx, KE, A["keysT"][0])
        V.hold(tok_x)
        S.hold(tok_x)

        modd = nc.dram_tensor("mod_scratch", (5, 6144), F32, kind="Internal").ap()
        t_sv = act(svb, cv, ACT.Sigmoid)
        t_sv = tt(svb, svb, cv, M, t_sv)
        mst = [Cell(sem(f"s_mst{i}")) for i in range(2)]
        mbi = [Cell(sem(f"s_mbi{i}")) for i in range(2)]
        mod_tok = {}

        def modvec(l, mem, js=range(12)):
            m = 2 if l < 2 else 1
            js = list(js)
            bb = [Slot(mem(512), mbi[i]) for i in range(2)]
            md = [Slot(mem(512), mst[i]) for i in range(2)]
            for x_ in (*bb, *md):
                x_.rel = everything()
            for i in range(2):
                md[i].rel = (md[i].rel, (mst[i].sem, mst[i].n))
            src = A["w_mod"][l] if l < 2 else A["ada_w_2"][0]
            bsrc = A["b_mod"][l:l + 1, :] if l < 2 else A["ada_b_2"][0:1, :]
            for j in js:
                b_, d_ = bb[j % 2], md[j % 2]
                cs = slice(512 * j, 512 * j + 512)
                tb = Y.dma(b_.cell, b_.ap[0:m, :], bsrc[0, cs].partition_broadcast(m), b_.rel)
                v = src[:, cs].rearrange("(p k) n -> p k n", k=8)
                s = wload([(lambda a: a.rearrange("p (k n) -> p k n", n=512), v)])
                w = s.ap.rearrange("p (k n) -> p k n", n=512)
                b = bank()
                for k in range(8):
                    c0 = 0 if l < 2 else 2
                    t = mm(b.ap[0:m, :], svb[:, k, c0:c0 + m], w[:, k, :], k == 0, k == 7, s.tok, t_sv, b.rel)
                s.rel = t
                b.rel = b_.rel = tt(d_.ap[0:m, :], b.ap[0:m, :], b_.ap[0:m, :], AD, t, tb, d_.rel)
                d_.rel = S.dma(d_.cell, modd[2 * l:2 * l + m, cs], d_.ap[0:m, :], b.rel)
                yield
            mod_tok[l] = (md[0].rel, md[1].rel)
            for q in ENG:
                q.hold(*mod_tok[l])

        def norm_stat(x, o, w, *after, junk):
            t = act(junk, x, ACT.Square, *after, accum=o)
            t = ts(o, o, 1.0 / w, 1e-6, M, AD, t)
            t = act(o, o, ACT.Sqrt, t)
            return recip(o, o, t)

        kv_ = {}
        o = 0
        for k in GROUP1:
            kv_[k] = KC[:, o:o + WIDTH[k]]
            o += WIDTH[k]
        kcos = kv_["cos"].rearrange("p (k n) -> p k n", n=256)
        ksin = kv_["sin"].rearrange("p (k n) -> p k n", n=256)
        kpool = kv_["pool"].rearrange("p (g k n) -> p g k n", g=4, k=2)
        krc = kv_["rcos"].rearrange("p (t a e) -> p t a e", t=2, a=2)
        krs = kv_["rsin"].rearrange("p (t a e) -> p t a e", t=2, a=2)

        def X(t):
            return XR[:, t, :] if t < 2 else CR[:, t - 2, :]

        bturn = [0]

        def brow(src, *after):
            s = bcs[bturn[0] % 4]
            bturn[0] += 1
            s.tok = S.dma(s.cell, s.ap, src.partition_broadcast(128), s.rel, after)
            return s

        def mrow(l, who, i):
            return brow(modd[2 * l + who, 1024 * i:1024 * i + 1024], mod_tok[l])

        def modulate(l, g, i0, who, HT):
            gr = brow(g)
            sc = mrow(l, who, i0 + 1)
            sh = mrow(l, who, i0)
            tg = stt(gr.ap, sc.ap, 1.0, gr.ap, AD, M, gr.tok, sc.tok)
            sc.rel = tg
            for n, t in enumerate((2 * who, 2 * who + 1)):
                a = norm_stat(X(t), small[:, t:t + 1], D, junk=H2[:, t, :])
                a = stt(H2[:, t, :], X(t), small[:, t:t + 1], gr.ap, M, M, a)
                a = tt(H2[:, t, :], H2[:, t, :], sh.ap, AD, sh.tok)
                for j in range(2):
                    b = bank()
                    for i in range(4):
                        u = tr(b.ap[:, 128 * i:128 * i + 128], H2[:, t, 512 * j + 128 * i:512 * j + 128 * i + 128], a, b.rel)
                    b.rel = copy(HT[:, 4 * j:4 * j + 4, 128 * n:128 * n + 128],
                                 b.ap.rearrange("p (i n) -> p i n", n=128), u, q=S)
                    yield
            gr.rel = sh.rel = a
            for q in (P, V, G):
                q.hold(S.last())

        def tok_major(s, n, dst, HTs):
            for i in range(2 * len(HTs)):
                HT = HTs[i // 2]
                b = bank()
                for k in range(8):
                    u = mm(b.ap[:, 0:n], HT[:, k, 128 * (i % 2):128 * (i % 2) + 128], s.w[:, k, 0:n], k == 0, k == 7, s.tok, b.rel)
                b.rel = copy(dst(i), b.ap[:, 0:n], u, q=(V, S)[i % 2])
                yield
            s.rel = u

        gsem = [Cell(sem(f"s_g{i}")) for i in range(8)]
        ND = NU = 4
        GK = 16
        gm = Mem((GR, BG))
        ds = [Slot(gm(D), gsem[i]) for i in range(ND)]
        us = [Slot(gm(D), gsem[4 + i]) for i in range(NU)]
        dg = [Slot(gm(128)) for _ in range(4)]
        AA = [Slot(gm(128)) for _ in range(2)]
        AW = [Slot(gm(128)) for _ in range(2)]
        tpb = gm(512)
        ready = {}
        cnt = [0, 0, 0]

        def peer_q(wq, HT, QA, t, m, shared, base):
            for blk in range(4):
                s = wblock(wq, 512 * blk, 512)
                for j in range(4):
                    b = bank()
                    for k in range(8):
                        u = mm(b.ap[:, 0:256], s.w[:, k, 128 * j:128 * j + 128], HT[:, k, :], k == 0, k == 7, s.tok, b.rel)
                    b.rel = copy(QA[:, 4 * blk + j, :], b.ap[:, 0:256], u, q=S)
                    yield
                s.rel = u
                P.hold(S.last())
                yield from peer_first(t, QA, m, shared, blk)
                if blk != 2:
                    yield from peer_pick(t, m, base, *((0, 2), (2, 4), None, (4, 8))[blk])

        def until(g, t):
            while (t, 0) not in ready:
                next(g)

        def peer_top(mem):
            m = dict(SV=mem(16, 16), SI=mem(16, 16, dt=U32), SF=mem(16, 16), tmp=mem(4, 128), CA=mem(8, 256),
                     TS=mem(8, 16), TP=mem(8, 16, dt=U32), TI=mem(2, 8, 16, dt=U32),
                     ES=mem(2, 8, 16), s8=mem(8), s8b=mem(8))
            m["TF"] = m["tmp"][:, 0:2, :].rearrange("p s (h k) -> p s h k", k=16)
            return m

        def weave(chains, cost, *after):
            prev = [V.last()] * len(chains)
            for fns in zip(*chains):
                for n, fn in enumerate(fns):
                    prev[n] = V(fn, prev[n], *after, free=True, cost=cost)
                after = ()
                yield

        def top16(v, ix, src, tmp):
            return [lambda e: e.max(v[:, 0:8], src),
                    lambda e: e.max_index(ix[:, 0:8], v[:, 0:8], src),
                    lambda e: e.match_replace(tmp, v[:, 0:8], src, NEG),
                    lambda e: e.max(v[:, 8:16], tmp),
                    lambda e: e.max_index(ix[:, 8:16], v[:, 8:16], tmp)]

        def peer_first(t, QA, m, shared, blk):
            b = bank()
            i = t % 2
            for j in range(4):
                hp = 4 * blk + j
                kt = KE[:, 128 * (hp % 2):128 * (hp % 2) + 128] if shared else KE[:, 128 * hp:128 * hp + 128]
                u = mm(b.ap[:, 128 * j:128 * j + 128], QA[:, hp, 128 * i:128 * i + 128], kt, True, True, b.rel)
            yield
            yield from weave([top16(m["SV"][:, 4 * blk + j, :], m["SI"][:, 4 * blk + j, :],
                                    b.ap[:, 128 * j:128 * j + 128], m["tmp"][:, j, :]) for j in range(4)], 0.25, u)
            b.rel = V.last()

        def peer_pick(t, m, base, ha, hb):
            SV, SI, SF, CA, TS_, TP, TI, TF, ES = (m[k] for k in ("SV", "SI", "SF", "CA", "TS", "TP", "TI", "TF", "ES"))
            n = hb - ha
            hs, h2 = slice(ha, hb), slice(2 * ha, 2 * hb)
            V(lambda e: e.tensor_copy(SF[:, h2, :], SI[:, h2, :]))
            sv = SV[:, h2, :].rearrange("p (h s) k -> p h s k", s=2)
            sf = SF[:, h2, :].rearrange("p (h s) k -> p h s k", s=2)
            ca = CA[:, hs, :].rearrange("p h (a b) -> p h a b", b=16)
            tt(ca, sv[:, :, 0, :].unsqueeze(3).to_broadcast([128, n, 16, 16]),
               sv[:, :, 1, :].unsqueeze(2).to_broadcast([128, n, 16, 16]), AD)
            yield
            for h0 in range(ha, hb, 4):
                yield from weave([top16(TS_[:, h, :], TP[:, h, :], CA[:, h, :], CA[:, h, :]) for h in range(h0, min(h0 + 4, hb))], 0.35)
            ts(TI[:, 0, hs, :], TP[:, hs, :], 4, None, ALU.logical_shift_right, None)
            ts(TI[:, 1, hs, :], TP[:, hs, :], 15, None, ALU.bitwise_and, None)
            V(lambda e: e.tensor_copy(TF[:, :, hs, :], TI[:, :, hs, :]))
            for s_ in range(2):
                tt(ca, TF[:, s_, hs, :].unsqueeze(3).to_broadcast([128, n, 16, 16]),
                   iota.unsqueeze(1).unsqueeze(1).to_broadcast([128, n, 16, 16]), ALU.is_equal)
                yield
                tt(ca, ca, sf[:, :, s_, :].unsqueeze(2).to_broadcast([128, n, 16, 16]), M)
                yield
                red(ES[:, s_, hs, :], ca, AD)
                yield
            e0 = ES[:, 0, hs, :]
            stt(e0, e0, 128.0, ES[:, 1, hs, :], M, AD)
            if base:
                ts(e0, e0, float(base), None, AD, None)
            ks = slice(16 * ha, 16 * hb)
            V(lambda e: e.tensor_copy(EI[:, t, ks], e0.rearrange("p h k -> p (h k)")))
            gt = GT[:, t, ks].rearrange("p (h k) -> p h k", k=16)
            t1 = tt(gt, TS_[:, hs, :], TS_[:, hs, 0:1].to_broadcast([128, n, 16]), SU)
            t1 = act(gt, gt, ACT.Exp, t1)
            red(m["s8"][:, hs], gt, AD, t1)
            recip(m["s8b"][:, hs], m["s8"][:, hs])
            a = tt(gt, gt, m["s8b"][:, hs].unsqueeze(2).to_broadcast([128, n, 16]), M)
            for h in range(ha, hb, 2):
                ready[t, h // 2] = a
            yield

        def peer_topk(t, QA, m, shared, base):
            for blk in range(4):
                yield from peer_first(t, QA, m, shared, blk)
            yield from peer_pick(t, m, base, 0, 8)

        def gather(tiles, table_d, table_u, gelu, gates):
            HP = psum[:, 0:D]
            ap, av = banks[2], banks[3]
            steps = [(n, g) for n in range(len(tiles)) for g in range(128 // GK)]
            state = {}

            def ups(n, g):
                t = tiles[n]
                for k in range(GK * g, GK * g + GK):
                    u_ = us[cnt[1] % NU]
                    cnt[1] += 1
                    tu = G.gather(u_.cell, u_.ap, table_u, EI[:, t, k:k + 1].bitcast(U32), u_.rel)
                    d_ = dg[cnt[2] % 4]
                    cnt[2] += 1
                    w = AW[n % 2].ap[:, k:k + 1]
                    td = act(d_.ap, ident, ACT.Copy, state[n, g], d_.rel, scale=w, free=True)
                    d_.rel = x = mm(ap.ap, d_.ap, u_.ap[:, 0:512], k == 0, k == 127, td, tu, ap.rel)
                    if k == 0:
                        y = V(lambda e, u_=u_, w=w: e.tensor_scalar(av.ap, u_.ap[:, 512:1024], w, None, M), tu, av.rel)

                    else:
                        y = stt(av.ap, u_.ap[:, 512:1024], w, av.ap, M, AD, tu, state[n], state[n, g], free=True)
                    state[n] = y
                    u_.rel = (x, y)
                    yield
                AW[n % 2].rel = (x, y)
                if g == 128 // GK - 1:
                    gr = gates()
                    X_ = X(t)
                    for c, b in enumerate((ap, av)):
                        cs = slice(512 * c, 512 * c + 512)
                        b.rel = tt(tpb, b.ap, gr.ap[:, cs], M, x, gr.tok)
                        tt(X_[:, cs], X_[:, cs], tpb, AD)
                    gr.rel = V.last()

            for s_, (n, g) in enumerate(steps):
                t = tiles[n]
                up = ups(*steps[s_ - 1]) if s_ else iter(())
                if GK * g % 32 == 0:
                    while (t, GK * g // 32) not in ready:
                        yield "more"
                    t_e = ready.pop((t, GK * g // 32))
                if g == 0:
                    for c in range(2):
                        th = copy(psum[:, 512 * c:512 * c + 512], H2[:, t, 512 * c:512 * c + 512], banks[0].rel, banks[1].rel, q=S)
                A_ = AA[n % 2]
                for k in range(GK * g, GK * g + GK):
                    d_ = ds[cnt[0] % ND]
                    cnt[0] += 1
                    tg = G.gather(d_.cell, d_.ap, table_d, EI[:, t, k:k + 1].bitcast(U32), d_.rel, t_e)
                    d_.rel = a = stt(d_.ap, d_.ap, 1.0, HP, M, M, tg, th, A_.rel, accum=A_.ap[:, k:k + 1], free=True)
                    yield
                    for _ in up:
                        yield
                        break
                yield from up
                banks[0].rel = banks[1].rel = a
                ks = slice(GK * g, GK * g + GK)
                w_ = AW[n % 2]
                a = act(w_.ap[:, ks], A_.ap[:, ks], gelu, a, w_.rel)
                A_.rel = a if g == 128 // GK - 1 else A_.rel
                state[n, g] = tt(w_.ap[:, ks], w_.ap[:, ks], GT[:, t, ks], M, a)
            yield from ups(*steps[-1])

        def small_weights(l):
            s = wload([(lambda a: a[:, 0:1536].rearrange("p (k n) -> p k n", n=768),
                        A["w_uq"][l].rearrange("(k p) n -> p k n", p=128)),
                       (lambda a: a[:, 1536:2560], A["w_ukv"][l]),
                       (lambda a: a[0:64, 2560:2816].rearrange("p (g d) -> p g d", g=4),
                        A["w_grp"][l].rearrange("g c d -> c g d"))])
            s.uq = s.ap[:, 0:1536].rearrange("p (k n) -> p k n", n=768)
            s.ukv = s.ap[:, 1536:2560]
            s.grp = s.ap[0:64, 2560:2816].rearrange("p (g d) -> p g d", g=4)
            return s

        def temps(mem):
            m = dict(qt=mem(768), kt=mem(768), kvt=mem(1024), junk=mem(256), rt=mem(3, 128), CQ=mem(2, 128), CK=mem(128))
            return m

        def qkv(l, t, z, m, sq, QT=None, KT=None, VV=None):
            cols = cols2[:, l, :]
            n = t % 2
            parts = ([(0, 256, "CQ", 24, 2)] if QT is not None else []) + ([(256, 128, "CK", 26, 1)] if KT is not None else [])
            for c0, w, name, col, nk in parts:
                zc = z[:, c0:c0 + w]
                a = norm_stat(zc, small[:, 8:9], w, V.last(), S.last(), junk=m["junk"][:, 0:w])
                a = ts(zc, zc, small[:, 8:9], None, M, None, a)
                b = bank()
                for k in range(nk):
                    u = tr(b.ap[:, 128 * k:128 * k + 128], zc[:, 128 * k:128 * k + 128], a, b.rel)
                for k in range(nk):
                    o_ = m["CQ"][:, k, :] if name == "CQ" else m["CK"]
                    b.rel = act(o_, b.ap[:, 128 * k:128 * k + 128], ACT.Copy, u, scale=cols[:, col + k:col + k + 1])
                yield
            tc = S.last()

            def rope(v, nh):
                x1, x2 = v[:, :, :, 0, :], v[:, :, :, 1, :]
                co = krc[:, t, :, :].unsqueeze(1).to_broadcast([128, nh, 2, 8])
                si = krs[:, t, :, :].unsqueeze(1).to_broadcast([128, nh, 2, 8])
                r = [m["rt"][:, i, 0:16 * nh].rearrange("p (h a e) -> p h a e", a=2, e=8) for i in range(3)]
                tt(r[0], x1, co, M)
                tt(r[1], x2, si, M)
                tt(r[2], x1, si, M)
                tt(x1, r[0], r[1], SU)
                tt(r[0], x2, co, M)
                return tt(x2, r[2], r[0], AD)

            if QT is not None:
                qt = m["qt"]
                for j in range(2):
                    b = bank()
                    for k in range(2):
                        u = mm(b.ap[:, 0:384], m["CQ"][:, k, :], sq.uq[:, k, 384 * j:384 * j + 384], k == 0, k == 1, tc, sq.tok, b.rel)
                    b.rel = copy(qt[:, 384 * j:384 * j + 384], b.ap[:, 0:384], u, q=V)
                yield
                qv = qt.rearrange("p (h c) -> p h c", c=96)
                if t < 2:
                    rope(qv[:, :, 64:96].rearrange("p h (a s e) -> p h a s e", a=2, s=2), 8)
                tq = V.last()
                for j in range(2):
                    b = bank()
                    for i in range(4):
                        u = tr(b.ap[0:96, 128 * i:128 * i + 128], qv[:, 4 * j + i, :], tq, b.rel)
                    b.rel = copy(QT[0:96, 4 * j:4 * j + 4, 128 * n:128 * n + 128],
                                 b.ap[0:96, :].rearrange("p (i n) -> p i n", n=128), u, q=S)
                V.hold(u)
                yield
            if KT is not None:
                kvt, kt = m["kvt"], m["kt"]
                for j in range(2):
                    b = bank()
                    u = mm(b.ap, m["CK"], sq.ukv[:, 512 * j:512 * j + 512], True, True, tc, sq.tok, b.rel)
                    b.rel = copy(kvt[:, 512 * j:512 * j + 512], b.ap, u, q=V)
                yield
                kr = z[:, 384:416]
                if t < 2:
                    rope(kr.rearrange("p (h a s e) -> p h a s e", h=1, a=2, s=2), 1)
                kv3 = kvt.rearrange("p (h c) -> p h c", c=128)
                kt3 = kt.rearrange("p (h c) -> p h c", c=96)
                V(lambda e: e.tensor_copy(kt3[:, :, 0:64], kv3[:, :, 0:64]))
                a = V(lambda e: e.tensor_copy(kt3[:, :, 64:96], kr.unsqueeze(1).to_broadcast([128, 8, 32])))
                V(lambda e: e.tensor_copy(VV[:, n, :].rearrange("p (h c) -> p h c", c=64), kv3[:, :, 64:128]))
                for j in range(2):
                    b = bank()
                    for i in range(4):
                        u = tr(b.ap[0:96, 128 * i:128 * i + 128], kt3[:, 4 * j + i, :], a, b.rel)
                    b.rel = copy(KT[0:96, 4 * j:4 * j + 4, 128 * n:128 * n + 128],
                                 b.ap[0:96, :].rearrange("p (i n) -> p i n", n=128), u, q=S)
                V.hold(u)
                yield
            sq.rel = P.last()

        def attend(QT, kvs, AT, PB, PT, at):
            rs, nm, mx = small[:, 16:24], small[:, 24:32], small[:, 32:40]
            nk = 2 * len(kvs)
            ring = ring_banks[0]
            ab = banks[ring[-1]]
            own_ring = [ring[:-1], 0]

            def bk():
                own_ring[1] += 1
                return banks[own_ring[0][own_ring[1] % len(own_ring[0])]]

            P.hold(ab.rel, V.last(), S.last())

            def scores(t, h):
                pb = PB[h % 2]
                b = bk()
                for i, (KT, _) in enumerate(kvs):
                    u = mm(b.ap[:, 256 * i:256 * i + 256], QT[0:96, h, 128 * t:128 * t + 128], KT[0:96, h, :], True, True, b.rel)
                yield
                r = red(mx[:, h:h + 1], b.ap[:, 0:128 * nk], ALU.max, u)
                a = ts(nm[:, h:h + 1], mx[:, h:h + 1], -ATT_SCALE, None, M, None, r)
                yield
                b.rel = pb.tok = act(pb.ap[:, 0:128 * nk], b.ap[:, 0:128 * nk], ACT.Exp, a, pb.rel, scale=ATT_SCALE,
                                     bias=nm[:, h:h + 1], accum=rs[:, h:h + 1])
                yield

            def values(t, h):
                pb, pt = PB[h % 2], PT[h % 2]
                b = bk()
                for i in range(nk):
                    u = tr(b.ap[:, 128 * i:128 * i + 128], pb.ap[:, 128 * i:128 * i + 128], pb.tok, b.rel)
                pb.rel = u
                yield
                b.rel = a = copy(pt.ap[:, 0:128 * nk], b.ap[:, 0:128 * nk], u, pt.rel, q=(V, S)[h % 2])
                yield
                for i in range(nk):
                    VV = kvs[i // 2][1]
                    u = mm(ab.ap[:, 64 * h:64 * h + 64], pt.ap[:, 128 * i:128 * i + 128], VV[:, i % 2, 64 * h:64 * h + 64], i == 0, i == nk - 1, a, ab.rel)
                pt.rel = u
                return u

            for t in range(2):
                for h in range(9):
                    if h < 8:
                        yield from scores(t, h)
                    if h > 0:
                        u = yield from values(t, h - 1)
                recip(rs, rs, S.last())
                ab.rel = a = tt(at.rearrange("p (h c) -> p h c", c=64), ab.ap.rearrange("p (h c) -> p h c", c=64),
                                rs.unsqueeze(2).to_broadcast([128, 8, 64]), M, u)
                S.hold(a)
                b = bk()
                for i in range(4):
                    u = tr(b.ap[:, 128 * i:128 * i + 128], at[:, 128 * i:128 * i + 128], a, b.rel)
                b.rel = copy(AT[:, :, 128 * t:128 * t + 128], b.ap.rearrange("p (i n) -> p i n", n=128), u, q=S)
                V.hold(u)
                yield
            P.hold(S.last())

        def spread(l, z, cz, pz, FT, PL, sq):
            cols = cols2[:, l, :]
            for f, km in enumerate((kcos, ksin)):
                for c in range(2):
                    b = bank()
                    for k in range(2):
                        u = mm(b.ap[:, 0:256], z[:, k, 416 + 128 * c:544 + 128 * c], km[:, k, :], k == 0, k == 1, b.rel)
                    b.rel = act(cz[:, f, c, :], b.ap[:, 0:256], ACT.Copy, u, scale=1.0 if f == 0 else -1.0)
                yield
            tz = S.last()
            for c in range(2):
                b = bank()
                n = 0
                for f, km in enumerate((kcos, ksin)):
                    for k in range(2):
                        u = mm(b.ap[:, 0:256], km[:, k, 128 * c:128 * c + 128], cz[:, f, k, :], n == 0, n == 3, tz, b.rel)
                        n += 1
                b.rel = copy(FT[:, c, :], b.ap[:, 0:256], u, q=V)
                yield
            for g in range(4):
                b = bank()
                for k in range(2):
                    u = mm(b.ap[0:64, 0:256], z[:, k, 672 + 64 * g:736 + 64 * g], kpool[:, g, k, :], k == 0, k == 1, b.rel)
                b.rel = copy(pz[:, g, :], b.ap[0:64, 0:256], u, q=S)
                yield
            tz = S.last()
            for g in range(4):
                r = slice(64 * (g % 2), 64 * (g % 2) + 64)
                b = bank()
                u = mm(b.ap[r, 0:256], sq.grp[:, g, :], pz[:, g, :], True, True, tz, sq.tok, b.rel)
                b.rel = ts(PL[r, g // 2, :], b.ap[r, 0:256], cols[r, 27 + g // 2:28 + g // 2], None, M, None, u)
            sq.rel = u
            P.hold(V.last())
            yield

        BR = {0: ("w_oa", 4), 1: ("w_ob", 2), 2: ("w_oc", 2)}

        def gates(l, HT, srcs, MX, gs, ty, ga=None):
            cols = cols2[:, l, :]
            for j in range(8):
                parts = [(lambda a, i=i: a[:, 1024 * i:1024 * i + 1024].rearrange("p (k n) -> p k n", n=128),
                          A["w_in"][l][:, 928 + 1024 * i + 128 * j:928 + 1024 * i + 128 * j + 128].rearrange("(k p) n -> p k n", p=128))
                         for i in range(3)]
                offs = {}
                o = 3072
                for i in srcs:
                    name, nk = BR[i]
                    parts.append((lambda a, o=o, nk=nk: a[:, o:o + 128 * nk].rearrange("p (k n) -> p k n", n=128),
                                  A[name][l][:, 128 * j:128 * j + 128].rearrange("(k p) n -> p k n", p=128)))
                    offs[i] = (o, nk)
                    o += 128 * nk
                s = wload(parts)
                first = True
                for i in range(3):
                    b = bank()
                    wg = s.ap[:, 1024 * i:1024 * i + 1024].rearrange("p (k n) -> p k n", n=128)
                    for k in range(8):
                        u = mm(b.ap[:, 0:256], wg[:, k, :], HT[:, k, :], k == 0, k == 7, s.tok, b.rel)
                    g_ = gs[i] if i in srcs else ga[:, j, :]
                    b.rel = a = act(g_, b.ap[:, 0:256], ACT.Sigmoid, u, V.last(), bias=cols[:, 8 * i + j:8 * i + j + 1])
                    yield
                    if i not in srcs:
                        continue
                    b = bank()
                    o, nk = offs[i]
                    wy = s.ap[:, o:o + 128 * nk].rearrange("p (k n) -> p k n", n=128)
                    for k in range(nk):
                        u = mm(b.ap[:, 0:256], wy[:, k, :], srcs[i][:, k, :], k == 0, k == nk - 1, b.rel)
                    if first:
                        b.rel = tt(MX[:, j, :], g_, b.ap[:, 0:256], M, a, u)
                    else:
                        b.rel = tt(ty, g_, b.ap[:, 0:256], M, a, u)
                        tt(MX[:, j, :], MX[:, j, :], ty, AD)
                    first = False
                    yield
                s.rel = u
            P.hold(V.last())

        def gate_first(l, AT, MX, ga, ty):
            v = A["w_oa"][l].rearrange("(k p) n -> p k n", p=128)
            s = wload([(lambda a: a.rearrange("p (k n) -> p k n", n=1024), v)])
            w = s.ap.rearrange("p (k n) -> p k n", n=1024)
            for j in range(8):
                b = bank()
                for k in range(4):
                    u = mm(b.ap[:, 0:256], w[:, k, 128 * j:128 * j + 128], AT[:, k, :], k == 0, k == 3, s.tok, b.rel)
                b.rel = tt(ty, ga[:, j, :], b.ap[:, 0:256], M, u)
                tt(MX[:, j, :], MX[:, j, :], ty, AD)
                yield
            s.rel = u
            P.hold(V.last())

        def project(w, g, who, MX, ty):
            for c in range(2):
                s = wblock(w, 512 * c, 512)
                for i in range(2):
                    b = bank()
                    for k in range(8):
                        u = mm(b.ap, MX[:, k, 128 * i:128 * i + 128], s.w[:, k, :], k == 0, k == 7, s.tok, b.rel)
                    b.rel = tt(ty, b.ap, g.ap[:, 512 * c:512 * c + 512], M, u, g.tok)
                    xs = X(2 * who + i)[:, 512 * c:512 * c + 512]
                    tt(xs, xs, ty, AD)
                    yield
                s.rel = u
            g.rel = V.last()
            S.hold(V.last())

        def zrows(t):
            return H2[:, t, 0:928]

        def zpair(who):
            return H2[:, 2 * who:2 * who + 2, 0:928]

        run(modvec(0, Mem((NB - 2048, NB)), range(4)))
        m0 = Mem((BG, NB))
        HTc, KTc, VVc = m0(8, 256), m0(8, 256), m0(2, 512)
        after_c = m0.free[0][0]
        QT = m0(8, 256)
        AFP = m0(8, 256)
        AT, FT, PL = AFP[:, 0:4, :], AFP[:, 4:6, :], AFP[:, 6:8, :]
        T0 = m0.free[0][0]
        mx_ = Mem((GR2, BG))
        HTx, KTx, VVx = mx_(8, 256), mx_(8, 256), mx_(2, 512)

        def start0():
            yield from modulate(0, A["norm1_g"][0], 0, 0, HTx)
            yield from modulate(0, A["norm1_g"][0], 0, 1, HTc)
            fence()
            for c0, n in ((0, 512), (512, 416)):
                s = wblock(A["w_in"][0], c0, n)
                yield from tok_major(s, n, lambda i: H2[:, i, c0:c0 + n], (HTx, HTc))
            fence()
            sq = small_weights(0)
            tm = temps(Mem((T0, NB)))
            for t in range(4):
                yield from qkv(0, t, zrows(t), tm, sq, QT if t < 2 else None, (KTx, KTc)[t // 2], (VVx, VVc)[t // 2])
            fence()

        def att_bufs(mem):
            return [Slot(mem(512)) for _ in range(2)], [Slot(mem(512)) for _ in range(2)], mem(512)

        def attend0(kvs):
            yield from attend(QT, kvs, AT, *att_bufs(Mem((T0, NB))))
            fence()

        def mix_rest(l, who, HT, HP):
            sq = small_weights(l)
            yield from spread(l, zpair(who), QT.rearrange("p (f c) n -> p f c n", c=2)[:, 0:2, :, :],
                              QT[0:64, 4:8, :], FT, PL, sq)
            fence()
            mem = Mem((T0, NB))
            gs, ty = [mem(256) for _ in range(3)], mem(256)
            yield from gates(l, HT, {0: AT, 1: FT, 2: PL}, QT, gs, ty)
            fence()
            mem = Mem((T0, NB))
            yield from project(A["w_out"][l], mrow(l, who, 2), who, QT, mem(512))
            fence()
            yield from modulate(l, A["norm2_g"][l], 3, who, HP)
            fence()

        def start1():
            yield from start0()
            yield from attend0([(KTx, VVx), (KTc, VVc)])

        together(start1(), modvec(0, Mem((NB - 2048, NB)), range(4, 12)), RATES[5], [0, 1], [2])
        pm = Mem((after_c, NB))
        QA = pm(16, 256)
        pt = peer_top(pm)
        HTp = pm(8, 256)
        run(mix_rest(0, 0, HTx, HTp))
        dump("x1_0", XR)
        wuse[0] = 2
        pq0 = peer_q(A["w_pq"][0], HTp, QA, 0, pt, False, 0)
        until(pq0, 0)

        def back0():
            yield FAST
            yield from pq0
            yield SLOW
            yield from peer_topk(1, QA, pt, False, 0)
            fence()
            tm = temps(Mem((T0, NB)))
            sq = small_weights(0)
            for t in (2, 3):
                yield from qkv(0, t, zrows(t), tm, sq, QT)
            fence()
            yield from attend0([(KTc, VVc)])
            yield from mix_rest(0, 1, HTc, HTc)
            yield from peer_q(A["w_pq"][0], HTc, QA, 2, pt, False, 0)
            yield from peer_topk(3, QA, pt, False, 0)

        def gate_row(l, who):
            return lambda: mrow(l, who, 5)

        TD, TU = A["peer_down"], A["peer_up"]
        together(gather([0, 1], TD, TU, ACT.Gelu_apprx_tanh, gate_row(0, 0)), back0(), RATES[0])
        dump("x2_0", XR)

        m1 = Mem((BG, NB))
        HTx, KTx, VVx = m1(8, 256), m1(8, 256), m1(2, 512)
        QT = m1(8, 256)
        AFP = m1(8, 256)
        AT, FT, PL = AFP[:, 0:4, :], AFP[:, 4:6, :], AFP[:, 6:8, :]
        L1T = m1.free[0][0]
        MX, ga = m1(8, 256), m1(8, 256)
        L1E = m1.free[0][0]

        def back1():
            yield from modvec(1, Mem((L1T, NB)))
            fence()
            yield from modulate(1, A["norm1_g"][1], 0, 0, HTx)
            fence()
            for c0, n in ((0, 512), (512, 416)):
                s = wblock(A["w_in"][1], c0, n)
                yield from tok_major(s, n, lambda i: H2[:, i, c0:c0 + n], (HTx,))
            fence()
            sq = small_weights(1)
            tm = temps(Mem((L1T, NB)))
            for t in (0, 1):
                yield from qkv(1, t, zrows(t), tm, sq, QT, KTx, VVx)
            fence()
            yield from spread(1, zpair(0), MX.rearrange("p (f c) n -> p f c n", c=2)[:, 0:2, :, :], MX[0:64, 4:8, :], FT, PL, sq)
            fence()
            mem = Mem((L1E, NB))
            gs, ty = [mem(256) for _ in range(3)], mem(256)
            yield from gates(1, HTx, {1: FT, 2: PL}, MX, gs, ty, ga)

        together(gather([2, 3], TD, TU, ACT.Gelu_apprx_tanh, gate_row(0, 1)), back1(), RATES[1])
        wslots[2].rel = everything()
        wuse[0] = 3
        dump("c2_0", CR)
        ck = Cell(sem("s_keys"))
        t_k = Y.dma(ck, KE, A["keysT"][1], everything())
        mx_ = Mem((GR2, BG))
        HTc, KTc, VVc = mx_(8, 256), mx_(8, 256), mx_(2, 512)
        def late1():
            yield from modulate(1, A["norm1_g"][1], 0, 1, HTc)
            fence()
            s = wblock(A["w_in"][1], 256, 160)
            yield from tok_major(s, 160, lambda i: H2[:, 2 + i, 256:416], (HTc,))
            fence()
            sq = small_weights(1)
            tm = temps(Mem((BG, BG + 2048), (L1E, NB)))
            for t in (2, 3):
                yield from qkv(1, t, zrows(t), tm, sq, None, KTc, VVc)
            fence()
            yield from attend(QT, [(KTx, VVx), (KTc, VVc)], AT, *att_bufs(Mem((BG, BG + 2048), (L1E, NB))))
            fence()

        run(late1())
        run(gate_first(1, AT, MX, ga, Mem((L1E, NB))(256)))
        fence()
        run(project(A["w_out"][1], mrow(1, 0, 2), 0, MX, Mem((L1E, NB))(512)))
        fence()
        run(modulate(1, A["norm2_g"][1], 3, 0, HTx))
        fence()
        P.hold(t_k)
        pm = Mem((BG + 2048, NB))
        QA = pm(16, 256)
        pt = peer_top(pm)
        wuse[0] = 2
        pq1 = peer_q(A["w_pq"][1], HTx, QA, 0, pt, False, 16384)
        until(pq1, 0)

        def back2():
            yield FAST
            yield from pq1
            yield SLOW
            yield from peer_topk(1, QA, pt, False, 16384)
            yield from modvec(2, pm)

        together(gather([0, 1], TD, TU, ACT.Gelu_apprx_tanh, gate_row(1, 0)), back2(), RATES[7])
        wslots[2].rel = everything()
        wuse[0] = 3

        fg = brow(A["final_g"])
        for t in range(2):
            a = norm_stat(XR[:, t, :], small[:, t:t + 1], D, junk=H2[:, t, :])
            stt(XR[:, t, :], XR[:, t, :], small[:, t:t + 1], fg.ap, M, M, a, fg.tok)
        fg.rel = V.last()
        S.hold(V.last())
        dump("xf", XR)
        K2 = arena[:, KCR:KCR + sum(WIDTH[k] for k in GROUP2)]
        o = 0
        k2 = {}
        for k in GROUP2:
            k2[k] = K2[:, o:o + WIDTH[k]]
            o += WIDTH[k]
        dist = k2["dist"].rearrange("p (k n) -> p k n", n=256)
        lcnt = k2["lcnt"].rearrange("p (k n) -> p k n", n=256)
        tri = k2["tri"].rearrange("p (k n) -> p k n", n=128)
        msk = k2["msk"].rearrange("p (k n) -> p k n", n=128)
        sel = k2["sel"].rearrange("p (k n) -> p k n", n=128)
        selT = k2["selT"].rearrange("p (k n) -> p k n", n=128)
        hb4 = k2["hblk"][:, 0:4].unsqueeze(1).unsqueeze(3).to_broadcast([128, 2, 4, 64])
        hbn4 = k2["hblk"][:, 4:8].unsqueeze(1).unsqueeze(3).to_broadcast([128, 2, 4, 64])
        fence()
        c2 = Cell(sem("s_const2"))
        Y.dma(c2, K2, A["k2"], everything())
        tk2 = Y.dma(c2, KE[:, 0:256], A["keysT_2"])
        HT = Mem((2048, 4096))(8, 256)
        run(modulate(2, A["norm1_g_2"][0], 0, 0, HT))
        zm = Mem((GR + 4096, NB))
        Z2 = zm(2, 3328)
        p1 = zm.free[0][0]
        ZP, ZN, MU = zm(2, 1792), zm(2, 1792), zm(2, 1792)
        G(lambda e: e.memset(ZP[0:1, 0, :], 0.0))
        t0 = G(lambda e: e.memset(ZN[:, 1, :], 0.0))
        cmu, csh, crw = Cell(sem("s_mu")), Cell(sem("s_shift")), Cell(sem("s_rows"))
        Y.dma(cmu, MU[:, 0, :], A["mu_prev_2"][0].partition_broadcast(128), everything())
        t_mu = Y.dma(cmu, MU[:, 1, :], A["mu_next_2"][0].partition_broadcast(128))
        MIX = H2[:, 2:4, :]
        R = slice(1536, 3328)

        def zblock(j, q=None):
            n = 512 if j < 6 else 256
            s = wblock(A["w_in_2"][0], 512 * j, n)
            for i in range(2):
                b = bank()
                for k in range(8):
                    u = mm(b.ap[:, 0:n], HT[:, k, 128 * i:128 * i + 128], s.w[:, k, 0:n], k == 0, k == 7, s.tok, b.rel)
                b.rel = copy(Z2[:, i, 512 * j:512 * j + n], b.ap[:, 0:n], u, q=q or (V, S)[i])
            s.rel = u

        for j in range(3, 7):
            zblock(j)
        tz = (V.last(), S.last(), t0)
        for t in range(2):
            Y.dma(csh, ZP[1:128, t, :], Z2[0:127, t, R], tz)
            Y.dma(csh, ZN[0:127, t, :], Z2[1:128, t, R])
        Y.dma(csh, ZP[0:1, 1, :], Z2[127:128, 0, R])
        tz = Y.dma(csh, ZN[127:128, 0, :], Z2[0:1, 1, R])
        for j in range(3):
            zblock(j, S)
        for t in range(2):
            z = Z2[:, t, R]
            tt(ZP[:, t, :], ZP[:, t, :], z, SU, tz, t_mu)
            tt(ZP[:, t, :], ZP[:, t, :], MU[:, 0, :], M)
            tt(ZN[:, t, :], ZN[:, t, :], z, SU, tz, t_mu, q=G)
            a = tt(ZN[:, t, :], ZN[:, t, :], MU[:, 1, :], M, q=G)
            tt(z, z, ZP[:, t, :], AD, a)
            tt(z, z, ZN[:, t, :], AD)
        marks = fence()
        dump("zr", Z2)
        rest = Mem((p1, NB))
        RW = rest(4736)
        rows = {}
        o = 0
        for name, n in (("lnx_g_2", 512), ("lnx_b_2", 512), ("k_k_2", 512), ("k_a_2", 512), ("r_k_2", 512),
                        ("w_decay0_2", 1024), ("a_gate0_2", 1024), ("q_norm_g_2", 64), ("k_norm_g_2", 64)):
            src = A[name][0]
            if name == "r_k_2":
                src = src.rearrange("h n -> (h n)")
            elif n == 1024:
                src = src.rearrange("a n -> (a n)")
            rows[name] = RW[:, o:o + n]
            t_rw = Y.dma(crw, rows[name], src.partition_broadcast(128), marks)
            o += n
        bcm = Mem((BCR, H2R))
        LW = bcm(5, 512)
        for d in range(2):
            Y.dma(crw, LW[0:64, d, :], A["w_decay_up_2"][0, d], marks)
            Y.dma(crw, LW[0:64, 2 + d, :], A["a_gate_up_2"][0, d])
        t_rw = Y.dma(crw, LW[:, 4, :], A["g_up_2"][0])
        QN, KN, BI = bcm(512), bcm(512), bcm(2, 256)
        wr = [arena[:, WR + 2048 * i:WR + 2048 * i + 2048] for i in range(4)] + [arena[:, GR + 2048 * i:GR + 2048 * i + 2048] for i in range(2)]
        AL, BE, KA, RO, PI = [w.rearrange("p (c h s) -> p c h s", c=8, h=8) for w in wr[:5]]
        GG = wr[5][:, 0:1024].rearrange("p (t n) -> p t n", n=512)
        BON = wr[5][:, 1024:2048].rearrange("p (t n) -> p t n", n=512)
        QT2 = arena[:, 2048:4096].rearrange("p (h n) -> p h n", n=256)
        p2 = rest.free[0][0]
        KT2 = rest(8, 256)
        p3 = rest.free[0][0]
        LT = rest(256)
        LTT = rest(3, 128)
        E_ = [rest(512) for _ in range(2)]
        A_ = [rest(512) for _ in range(2)]
        KKA = [rest(512) for _ in range(2)]
        KD = [rest(512) for _ in range(2)]
        KK, T1, T2 = rest(512), rest(512), rest(512)
        PB = [Slot(rest(256)) for _ in range(2)]
        PT = [Slot(rest(256)) for _ in range(2)]
        s8, s8b = small[:, 40:48], small[:, 48:56]
        CE = math.exp(-0.5)

        def h3(a):
            return a.rearrange("p (h n) -> p h n", n=64)

        def b8(a):
            return a.unsqueeze(2).to_broadcast([128, 8, 64])

        def attend2():
            ss, mx, nm, rs = small[:, 0:8], small[:, 8:16], small[:, 16:24], small[:, 24:32]
            for t in range(2):
                for c0, dst, g, tr_ in ((0, QN, "q_norm_g_2", QT2), (512, KN, "k_norm_g_2", KT2)):
                    z = Z2[:, t, c0:c0 + 512]
                    d3 = dst.rearrange("p (h n) -> p h n", n=64)
                    tt(dst, z, z, M, t_rw)
                    red(ss, d3, AD)
                    a = ts(ss, ss, 1.0 / 64, 1e-6, M, AD)
                    a = act(ss, ss, ACT.Sqrt, a)
                    recip(ss, ss, a)
                    tt(d3, z.rearrange("p (h n) -> p h n", n=64), ss.unsqueeze(2).to_broadcast([128, 8, 64]), M)
                    a = tt(d3, d3, rows[g].unsqueeze(1).to_broadcast([128, 8, 64]), M)
                    for j in range(2):
                        b = bank()
                        for i in range(4):
                            h = 4 * j + i
                            u = tr(b.ap[0:64, 128 * i:128 * i + 128], dst[:, 64 * h:64 * h + 64], a, b.rel)
                        b.rel = copy(tr_[0:64, 4 * j:4 * j + 4, 128 * t:128 * t + 128],
                                     b.ap[0:64, :].rearrange("p (i n) -> p i n", n=128), u, q=S)
                    V.hold(u)
                    yield
            tq = S.last()
            ring = ring_banks[0][:-1]
            ab = banks[ring_banks[0][-1]]
            tn = [0]

            def bk():
                tn[0] += 1
                return banks[ring[tn[0] % len(ring)]]

            P.hold(ab.rel)
            def scores(t, h):
                pb = PB[h % 2]
                b = bk()
                u = mm(b.ap[:, 0:256], QT2[0:64, h, 128 * t:128 * t + 128], KT2[0:64, h, :], True, True, tq, b.rel)
                bi = BI[:, h % 2, :]
                stt(bi, dist[:, t, :], 2.0 ** -(h + 1), lcnt[:, t, :], M, AD, pb.bi)
                yield
                r = b.rel = stt(bi, b.ap[:, 0:256], 0.125, bi, M, AD, u)
                red(mx[:, h:h + 1], bi, ALU.max)
                a = ts(nm[:, h:h + 1], mx[:, h:h + 1], -1.0, None, M, None)
                yield
                pb.bi = pb.tok = act(pb.ap, bi, ACT.Exp, a, pb.rel, bias=nm[:, h:h + 1], accum=rs[:, h:h + 1])
                yield

            def values(t, h):
                pb, pt = PB[h % 2], PT[h % 2]
                b = bk()
                for i in range(2):
                    u = tr(b.ap[:, 128 * i:128 * i + 128], pb.ap[:, 128 * i:128 * i + 128], pb.tok, b.rel)
                pb.rel = u
                yield
                b.rel = a = copy(pt.ap, b.ap[:, 0:256], u, pt.rel, q=S)
                yield
                for i in range(2):
                    u = mm(ab.ap[:, 64 * h:64 * h + 64], pt.ap[:, 128 * i:128 * i + 128],
                           Z2[:, i, 1024 + 64 * h:1088 + 64 * h], i == 0, i == 1, a, ab.rel)
                pt.rel = u
                yield
                return u

            PB[0].bi = PB[1].bi = ()
            for t in range(2):
                for h in range(9):
                    if h < 8:
                        yield from scores(t, h)
                    if h > 0:
                        u = yield from values(t, h - 1)
                recip(rs, rs, S.last())
                ab.rel = tt(MIX[:, t, 0:512].rearrange("p (h c) -> p h c", c=64), ab.ap.rearrange("p (h c) -> p h c", c=64),
                            rs.unsqueeze(2).to_broadcast([128, 8, 64]), M, u)
                S.hold(ab.rel)
                yield

        def recur():
            for t in range(2):
                r_, k_, v_ = (Z2[:, t, 1536 + 512 * i:2048 + 512 * i] for i in range(3))
                act(LT[:, 0:64], Z2[:, t, 3072:3136], ACT.Tanh)
                copy(LT[:, 64:128], Z2[:, t, 3136:3200], q=S)
                a = act(LT[:, 128:256], Z2[:, t, 3200:3328], ACT.Sigmoid)
                b = bank()
                tr(b.ap[0:64, 0:128], LT[:, 0:64], a, b.rel)
                tr(b.ap[0:64, 128:256], LT[:, 64:128])
                u = tr(b.ap[:, 256:384], LT[:, 128:256])
                yield
                copy(LTT[0:64, 0:2, :], b.ap[0:64, 0:256].rearrange("p (a n) -> p a n", n=128), u, q=S)
                b.rel = a = copy(LTT[:, 2, :], b.ap[:, 256:384], q=S)
                b = bank()
                u = mm(b.ap, LTT[:, 2, :], LW[:, 4, :], True, True, a, b.rel)
                b.rel = copy(GG[:, t, :], b.ap, u, q=S)
                ts_ = []
                for d in range(2):
                    yield
                    b = bank()
                    u = mm(b.ap, LTT[0:64, 0, :], LW[0:64, d, :], True, True, b.rel)
                    b.rel = x = tt(E_[d], b.ap, rows["w_decay0_2"][:, 512 * d:512 * d + 512], AD, u)
                    act(E_[d], E_[d], ACT.Sigmoid, x)
                    b = bank()
                    u = mm(b.ap, LTT[0:64, 1, :], LW[0:64, 2 + d, :], True, True, b.rel)
                    b.rel = x = tt(A_[d], b.ap, rows["a_gate0_2"][:, 512 * d:512 * d + 512], AD, u)
                    ta = act(A_[d], A_[d], ACT.Sigmoid, x)
                yield
                tt(KK, k_, rows["k_k_2"], M)
                tt(T1, KK, KK, M)
                red(s8, h3(T1), AD)
                a = ts(s8, s8, 1e-12, None, ALU.max, None)
                a = act(s8, s8, ACT.Sqrt, a)
                recip(s8, s8, a)
                tt(h3(KK), h3(KK), b8(s8), M)
                for d in range(2):
                    tt(KKA[d], KK, A_[d], M, ta)
                    stt(KD[d], A_[d], -1.0, rows["k_a_2"], AD, M)
                    tkk = stt(KD[d], KD[d], 1.0, k_, AD, M)
                tt(T1, A_[0], A_[1], AD)
                ts(T1, T1, 0.5, -1.0, M, AD)
                tt(T1, T1, rows["k_a_2"], M)
                stt(T1, T1, 1.0, k_, AD, M)
                tt(T1, T1, r_, M)
                tt(T1, T1, rows["r_k_2"], M)
                red(s8b, h3(T1), AD)
                tt(h3(BON[:, t, :]), h3(v_), b8(s8b), M)
                yield
                for hf in range(2):
                    def cum(i0):
                        b = bank()
                        for d in range(2):
                            for i in range(4):
                                h = 4 * hf + i
                                u = mm(b.ap[64 * d:64 * d + 64, 128 * i:128 * i + 128], E_[d][:, 64 * h:64 * h + 64],
                                       tri[:, i0 + d, :], True, True, ta, b.rel)
                        return b, u

                    def turned(srcs):
                        b = bank()
                        for d in range(2):
                            for i in range(4):
                                h = 4 * hf + i
                                u = mm(b.ap[64 * d:64 * d + 64, 128 * i:128 * i + 128], srcs[d][:, 64 * h:64 * h + 64],
                                       ident, True, True, tkk, b.rel)
                        return b, u

                    def at4(w):
                        return w[:, 4 * t:4 * t + 4, 4 * hf:4 * hf + 4, :].rearrange("p c h s -> p h c s")

                    def v4(a):
                        return a.rearrange("p (h c s) -> p h c s", h=4, c=4)

                    S.hold(V.last())
                    b, u = cum(0)
                    act(at4(PI), v4(b.ap), ACT.Exp, u, scale=-CE)
                    b.rel = act(T1, b.ap, ACT.Exp, scale=CE)
                    yield
                    b, u = cum(2)
                    yield
                    b.rel = x = act(T2, b.ap, ACT.Exp, u, scale=-CE)
                    for srcs, dst, f in (((KK, KK), AL, v4(T2)), (KKA, BE, v4(T1)), (KD, KA, v4(T1)),
                                         ((r_, r_), RO, at4(PI))):
                        b, u = turned(srcs)
                        yield
                        b.rel = tt(at4(dst), f, v4(b.ap), M, u, x)
                S.hold(V.last(), P.last())
                V.hold(P.last())


        P.hold(t_rw, tk2)
        V.hold(t_rw, tk2)
        FRONT[0], BACK[0] = [0, 1, 2], [3, 4, 5, 6]
        zc = GR + 4096
        early = Mem((BCR, BCR + 2560), (p1 + 1024, p1 + 4608), (p3, p3 + 6272))
        late = Mem((2048, 4096), (BCR + 2560, H2R), (zc, zc + 2560), (zc + 3328, zc + 3328 + 2560), (p2, p2 + 2048), (p3 + 6272, NB))

        def batch_bufs(mem):
            return [dict(rb=mem(4, 128), rk=mem(4, 128), tl=mem(4, 128), br=mem(4, 64), kr=mem(4, 64), ve=mem(4, 256)) for d in range(2)]

        TMP = [early(4, 128) for _ in range(9)]
        LK, AR = early(4, 128), early(4, 64)
        PD = [batch_bufs(early), batch_bufs(late)]
        TA = [early(4, 128), late(4, 128)]
        ST = late(512)
        UE = [late(2, 4, 64) for _ in range(2)]
        YE = [late(2, 4, 64) for _ in range(2)]
        S1, S2 = late(512), late(512)
        left = {0: 8, 1: 8}

        def v128(a):
            return a.rearrange("p (n i) -> p n i", i=128)

        def g4(a):
            return a.rearrange("p (g h v) -> p g h v", g=2, h=4)

        def prep(bf, d, chunks):
            q = PD[bf][d]
            pr = slice(64 * d, 64 * d + 64)
            units = [(c, g) for c in chunks for g in range(2)]

            def part(w, c, g):
                return w[pr, c, 4 * g:4 * g + 4, :].rearrange("p h s -> p (h s)")

            def four(f, *after):
                b = bank()
                for n, (c, g) in enumerate(units):
                    u = f(b.ap, n, c, g, after, b.rel)
                return b, u

            def pair(l, r, masks):
                b, u = four(lambda o_, n, c, g, *w: mm(o_[:, 128 * n:128 * n + 128], part(l, c, g), part(r, c, g), True, True, *w))
                for mi, dst in masks:
                    b.rel = tt(dst, v128(b.ap), msk[:, mi, :].unsqueeze(1).to_broadcast([128, 4, 128]), M, u)
                return b.rel

            L, Mt, L2, M2, L4, M4, L8, Q, LO = TMP
            pair(AL, BE, ((d, L), (4 + d, LO)))
            pair(BE, AL, ((1 - d, Mt),))
            yield
            tQ = tt(Q, ident.unsqueeze(1).to_broadcast([128, 4, 128]), Mt, SU)

            def prod(l, r, *after):
                return four(lambda o_, n, c, g, *w: mm(o_[:, 128 * n:128 * n + 128], l[:, n, :], r[:, n, :], True, True, *w), *after)

            def power(l, r, dst, *after):
                b, u = prod(l, r, *after)
                b.rel = copy(dst, v128(b.ap), u, q=S)
                return b.rel

            power(Mt, L, L2, tQ)
            x = power(L, Mt, M2, tQ)
            yield
            pair(AL, KA, ((6 + d, LK),))
            power(M2, L2, L4, x)
            y = power(L2, M2, M4, x)
            yield
            pair(BE, RO, ((3 - d, q["rb"]),))
            z = power(M4, L4, L8, y)
            pair(KA, RO, ((3 - d, q["rk"]),))
            yield
            idn = ident[pr, 64 * d:64 * d + 64]
            rows_ = [(AL, AR), (BE, q["br"]), (KA, q["kr"])]
            for l, w in ((L2, x), (L4, y), (L8, z)):
                b, u = prod(l, Q, w, tQ)
                b.rel = tQ = tt(Q, Q, v128(b.ap), AD, u)
                src, dst = rows_.pop()
                b, u = four(lambda o_, n, c, g, *w_: mm(o_[:, 64 * n:64 * n + 64], part(src, c, g), idn, True, True, *w_))
                ta = b.rel = copy(dst, b.ap[:, 0:256].rearrange("p (n i) -> p n i", i=64), u, q=S)
                yield
            X1, QT_ = L2, M2
            b, u = prod(LO, Q, tQ)
            x = b.rel = copy(X1, v128(b.ap), u, q=S)
            b, u = four(lambda o_, n, c, g, *w: tr(o_[:, 128 * n:128 * n + 128], Q[:, n, :], *w), tQ)
            y = b.rel = copy(QT_, v128(b.ap), u, q=S)
            ve = q["ve"]
            for ci, c in enumerate(chunks):
                b = bank()
                u = mm(b.ap, selT[:, c % 4, :], Z2[:, c // 4, 2560:3072], True, True, b.rel)
                b.rel = tt(ve[:, 2 * ci:2 * ci + 2, :].rearrange("p g (h v) -> p g h v", h=4), g4(b.ap), hb4, M, u)
            yield
            b, u = prod(QT_, X1, x, y)
            b.rel = tQ = tt(Q, Q, v128(b.ap), SU, u)
            b, u = four(lambda o_, n, c, g, *w: mm(o_[pr, 128 * n:128 * n + 128], AR[:, n, :], Q[:, n, :], True, True, *w), tQ, ta)
            b.rel = copy(TA[bf][pr, :, :], v128(b.ap[pr, :]), u, q=S)
            b, u = prod(LK, Q, tQ)
            b.rel = copy(q["tl"], v128(b.ap), u, q=S)
            V.hold(u)
            S.hold(u)
            yield

        def steps(bf, chunks):
            for ci in range(2):
                st = {}
                for d in range(2):
                    q, pr = PD[bf][d], slice(64 * d, 64 * d + 64)
                    b = bank()
                    for g in range(2):
                        n, cs = 2 * ci + g, slice(256 * g, 256 * g + 256)
                        mm(b.ap[:, cs], TA[bf][pr, n, :], ST[pr, cs], True, False, V.last(), b.rel)
                        u = mm(b.ap[:, cs], q["tl"][:, n, :], q["ve"][:, n, :], False, True)
                    b.rel = st[d] = tt(UE[d], g4(b.ap), hbn4, M, u)
                    yield
                for d in range(2):
                    q, pr, c = PD[bf][d], slice(64 * d, 64 * d + 64), chunks[d][ci]
                    b2, b3 = bank(), bank()
                    for g in range(2):
                        n, cs = 2 * ci + g, slice(256 * g, 256 * g + 256)
                        ug = UE[d][:, g, :, :].rearrange("p h v -> p (h v)")
                        mm(b3.ap[:, cs], RO[pr, c, 4 * g:4 * g + 4, :].rearrange("p h s -> p (h s)"), ST[pr, cs], True, False, b3.rel)
                        mm(b3.ap[:, cs], q["rb"][:, n, :], ug, False, False, st[d])
                        u3 = mm(b3.ap[:, cs], q["rk"][:, n, :], q["ve"][:, n, :], False, True)
                    for g in range(2):
                        n, cs = 2 * ci + g, slice(256 * g, 256 * g + 256)
                        ug = UE[d][:, g, :, :].rearrange("p h v -> p (h v)")
                        mm(b2.ap[pr, cs], q["br"][:, n, :], ug, True, False, b2.rel)
                        u = mm(b2.ap[pr, cs], q["kr"][:, n, :], q["ve"][:, n, :], False, True)
                    b2.rel = tt(ST[pr, :], ST[pr, :], b2.ap[pr, :], AD, u)
                    pc = PI[pr, c, :, 31 if d == 0 else 0]
                    tt(h3(ST[pr, :]), h3(ST[pr, :]), pc.unsqueeze(2).to_broadcast([64, 8, 64]), M)
                    b3.rel = x = tt(YE[d], g4(b3.ap), hb4, M, u3)
                    ti = c // 4
                    left[ti] -= 1
                    u = mm(banks[6 + ti].ap, sel[:, c % 4, :], YE[d].rearrange("p g h v -> p (g h v)"),
                           left[ti] == 7, left[ti] == 0, x, banks[6 + ti].rel)
                    V.hold(u)
                    yield

        def preps(bt):
            for d, ch in enumerate(([2 * bt, 2 * bt + 1], [7 - 2 * bt, 6 - 2 * bt])):
                yield from prep(bt % 2, d, ch)


        def front2():
            yield from recur()
            fence()
            yield from preps(0)

        together(front2(), attend2(), RATES[3])
        memset(V, ST, 0.0)
        ring_banks[0] = [0, 1, 2, 3, 4, 5]
        FRONT[0], BACK[0] = [0, 1, 2], [3, 4, 5]
        for bt in range(4):
            ch = ([2 * bt, 2 * bt + 1], [7 - 2 * bt, 6 - 2 * bt])
            together(steps(bt % 2, ch), preps(bt + 1) if bt < 3 else None, RATES[4])
        FRONT[0], BACK[0] = [0, 1, 2, 3], [4, 5, 6, 7]
        fence()
        for t in range(2):
            yb = banks[6 + t]
            y3 = h3(yb.ap)
            red(s8, y3, AD)
            ts(s8, s8, 1.0 / 64, None, M, None)
            yb.rel = tt(h3(S2), y3, b8(s8), SU)
            tt(S1, S2, S2, M)
            red(s8, h3(S1), AD)
            a = ts(s8, s8, 1.0 / 64, 64e-5, M, AD)
            a = act(s8, s8, ACT.Sqrt, a)
            recip(s8, s8, a)
            tt(h3(S2), h3(S2), b8(s8), M)
            tt(S2, S2, rows["lnx_g_2"], M)
            tt(S2, S2, rows["lnx_b_2"], AD)
            tt(S2, S2, BON[:, t, :], AD)
            a = tt(MIX[:, t, 512:1024], S2, GG[:, t, :], M)
            for j in range(2):
                b = bank()
                for i in range(4):
                    u = tr(b.ap[:, 128 * i:128 * i + 128], MIX[:, t, 512 * j + 128 * i:512 * j + 128 * i + 128], a, b.rel)
                b.rel = copy(HT[:, 4 * j:4 * j + 4, 128 * t:128 * t + 128], b.ap.rearrange("p (i n) -> p i n", n=128), u, q=S)
        ring_banks[0] = list(range(8))
        marks = fence()
        dump("mix", MIX)
        for s in wslots + bcs:
            s.rel = (s.rel, everything())
        run(project(A["w_out_2"][0], mrow(2, 0, 2), 0, HT, Mem((BG, NB))(512)))
        fence()
        dump("x3", XR)
        run(modulate(2, A["norm2_g_2"][0], 3, 0, HT))
        fence()
        P.hold(tk2)
        pm = Mem((BG, NB))
        QA = pm(16, 256)
        pt = peer_top(pm)
        wuse[0] = 2
        pq2 = peer_q(A["peer_w_query_2"][0], HT, QA, 0, pt, True, 0)
        until(pq2, 0)

        def back3():
            yield FAST
            yield from pq2
            yield SLOW
            yield from peer_topk(1, QA, pt, True, 0)

        together(gather([0, 1], A["peer_u_2"], A["peer_v_2"], ACT.Gelu, lambda: mrow(2, 0, 5)),
                 back3(), RATES[2])
        for t in range(2):
            Y.dma(cout, out[0, 128 * t:128 * t + 128, :], XR[:, t, :], everything())

        block = ctx.enter_context(nc.Block())

        @block.vector
        def _(eng):
            V.play(eng)

        @block.scalar
        def _(eng):
            S.play(eng)

        @block.tensor
        def _(eng):
            P.play(eng)

        @block.gpsimd
        def _(eng):
            G.play(eng)

        @block.sync
        def _(eng):
            Y.play(eng)
            for c in (cout, *mst, cdbg):
                if c is not None and c.n:
                    eng.wait_ge(c.sem, c.n)


_NAMES = ["x", "ctx", "w_mod", "b_mod", "norm1_g", "norm2_g", "w_in", "w_uq", "w_ukv", "w_oa", "w_ob", "w_grp",
          "w_oc", "w_out", "w_pq", "final_g", "ada_w_2", "ada_b_2", "norm1_g_2", "w_in_2", "mu_prev_2",
          "mu_next_2", "q_norm_g_2", "k_norm_g_2", "w_decay0_2", "w_decay_up_2", "a_gate0_2", "a_gate_up_2",
          "g_up_2", "k_k_2", "k_a_2", "r_k_2", "lnx_g_2", "lnx_b_2", "w_out_2", "norm2_g_2", "peer_w_query_2"]


def layout(inputs):
    f = {k: np.ascontiguousarray(inputs[k]) for k in _NAMES}
    f["peer_down"] = np.asarray(inputs["peer_down"]).reshape(2 * 16384, D)
    f["peer_up"] = np.asarray(inputs["peer_up"]).reshape(2 * 16384, D)
    f["peer_u_2"] = np.asarray(inputs["peer_u_2"]).reshape(16384, D)
    f["peer_v_2"] = np.asarray(inputs["peer_v_2"]).reshape(16384, D)
    vecs = [np.asarray(inputs[k]).reshape(128, 8) for k in ("c", "c_ctx", "c_2")]
    f["cvec"] = np.ascontiguousarray(np.stack(vecs, -1).reshape(128, 24))
    f["cols"] = np.ascontiguousarray(np.concatenate(
        [np.asarray(inputs[k]).reshape(2, n, 128).transpose(0, 2, 1)
         for k, n in (("b_gate", 24), ("q_norm_g", 2), ("kv_norm_g", 1), ("pool_scale", 2))], 2))
    f["keysT"] = np.ascontiguousarray(np.asarray(inputs["peer_keys"]).transpose(0, 4, 1, 2, 3).reshape(2, 128, 2048))
    f["keysT_2"] = np.ascontiguousarray(np.concatenate(
        [np.asarray(inputs["peer_sub_keys1_2"])[0].T, np.asarray(inputs["peer_sub_keys2_2"])[0].T], 1))
    c = const_tables()
    for name, group in (("k0", GROUP0), ("k1", GROUP1), ("k2", GROUP2)):
        f[name] = np.ascontiguousarray(np.concatenate([c[k] for k in group], 1))
    return f


def build(nc, arrays, debug=None):
    A = {k: nc.dram_tensor("in_" + k, a.shape, mybir.dt.from_np(a.dtype), kind="ExternalInput").ap()
         for k, a in arrays.items()}
    out = nc.dram_tensor("out_x", (1, 256, D), F32, kind="ExternalOutput").ap()
    dbg = None
    if debug:
        dbg = {k: nc.dram_tensor("dbg_" + k, s, F32, kind="ExternalOutput").ap() for k, s in debug.items()}
    program(nc, A, out, dbg)


def kernel(**inputs):
    import concourse.bacc as bacc
    from concourse.bass_utils import run_bass_kernel_spmd

    arrays = layout(inputs)
    nc = bacc.Bacc("TRN2", target_bir_lowering=False, num_devices=1)
    build(nc, arrays)
    r = run_bass_kernel_spmd(nc, [{"in_" + k: a for k, a in arrays.items()}], core_ids=[0])
    return r.results[0]["out_x"]
```
